# Optimizing a Trainium2 kernel written in Bass

```python
import jax, jax.numpy as jnp
from jax import lax
import numpy as np

D_MODEL = 1024
BATCH = 1
SEQ = 1024
DEPTH = 2

RET_HEADS = 4
RET_DK = 128
RET_DV = 256
RET_CHUNK = 128
RET_QK_W = RET_HEADS * RET_DK
RET_V_W = RET_HEADS * RET_DV
DN_HEADS = 8
DN_DK = 128
DN_DV = 128
DN_CHUNK = 64
DN_QK_W = DN_HEADS * DN_DK
DN_V_W = DN_HEADS * DN_DV
CONV_K = 4
CONV_W = 2 * DN_QK_W + DN_V_W
ROPE_BASE = 10000.0
EPS = 1e-6

SPLITS = (RET_QK_W, RET_QK_W, RET_V_W, RET_V_W,
          DN_QK_W, DN_QK_W, DN_V_W, DN_V_W, DN_HEADS, DN_HEADS,
          D_MODEL, D_MODEL)
IN_W = sum(SPLITS)

kernel_name = "hybrid_retention_gated_deltanet_parallel"

def _split_points():
    pts, acc = [], 0
    for s in SPLITS[:-1]:
        acc += s
        pts.append(acc)
    return pts

def rmsnorm(x, g):
    xf = x.astype(jnp.float32)
    y = xf * lax.rsqrt(jnp.mean(xf * xf, axis=-1, keepdims=True) + EPS) * g.astype(jnp.float32)
    return y.astype(x.dtype)

def rope(x, pos):
    half = x.shape[-1] // 2
    inv_freq = jnp.power(ROPE_BASE, -jnp.arange(half, dtype=jnp.float32) / half)
    ang = pos.astype(jnp.float32)[:, None] * inv_freq[None, :]
    cos = jnp.cos(ang)[None, :, None, :]
    sin = jnp.sin(ang)[None, :, None, :]
    x1, x2 = x[..., :half], x[..., half:]
    return jnp.concatenate([x1 * cos - x2 * sin, x2 * cos + x1 * sin], axis=-1)

def l2norm(x):
    return x * lax.rsqrt(jnp.sum(x * x, axis=-1, keepdims=True) + EPS)

def causal_conv(x, w):
    c = x.shape[-1]
    return lax.conv_general_dilated(x, w[:, None, :].astype(x.dtype), window_strides=(1,),
                                    padding=[(CONV_K - 1, 0)],
                                    dimension_numbers=('NWC', 'WIO', 'NWC'),
                                    feature_group_count=c)

def retention(q, k, v):
    B, S, H, DK = q.shape
    DV = v.shape[-1]
    C = RET_CHUNK
    N = S // C
    log_g = jnp.log1p(-jnp.power(2.0, -5.0 - jnp.arange(H, dtype=jnp.float32)))
    idx = jnp.arange(C, dtype=jnp.float32)
    rel = idx[:, None] - idx[None, :]
    intra = jnp.where(rel[None] >= 0,
                      jnp.exp(jnp.maximum(rel, 0.0)[None] * log_g[:, None, None]), 0.0)
    q = q.reshape(B, N, C, H, DK)
    k = k.reshape(B, N, C, H, DK)
    v = v.reshape(B, N, C, H, DV)
    scores = jnp.einsum('bnihd,bnjhd->bnhij', q, k) * intra
    inner = jnp.einsum('bnhij,bnjhe->bnihe', scores, v)
    k_dec = k * jnp.exp((C - 1 - idx)[:, None] * log_g[None, :])[:, :, None]
    kv = jnp.einsum('bnjhd,bnjhe->nbhde', k_dec, v)
    chunk_decay = jnp.exp(C * log_g)[:, None, None]

    def step(state, kv_n):
        return state * chunk_decay + kv_n, state

    _, state_start = lax.scan(step, jnp.zeros((B, H, DK, DV), jnp.float32), kv)
    q_dec = q * jnp.exp((idx + 1.0)[:, None] * log_g[None, :])[:, :, None]
    cross = jnp.einsum('bnihd,nbhde->bnihe', q_dec, state_start)
    return (inner + cross).reshape(B, S, H, DV)

def gated_deltanet(q, k, v, beta, g):
    B, S, H, DK = q.shape
    DV = v.shape[-1]
    C = DN_CHUNK
    N = S // C
    to_chunks = lambda t: t.transpose(0, 2, 1, 3).reshape(B, H, N, C, t.shape[-1])
    q, k, v = to_chunks(q), to_chunks(k), to_chunks(v)
    beta = beta.transpose(0, 2, 1).reshape(B, H, N, C)
    gc = jnp.cumsum(g.transpose(0, 2, 1).reshape(B, H, N, C), axis=-1)
    idx = jnp.arange(C)
    causal = idx[:, None] >= idx[None, :]
    strict = idx[:, None] > idx[None, :]
    diff = gc[..., :, None] - gc[..., None, :]
    decay = jnp.exp(jnp.where(causal, diff, -jnp.inf))
    k_beta = k * beta[..., None]
    L = jnp.where(strict, jnp.einsum('bhncd,bhnjd->bhncj', k_beta, k) * decay, 0.0)
    a = L + jnp.eye(C, dtype=jnp.float32)
    rhs = jnp.concatenate([v * beta[..., None], k_beta * jnp.exp(gc)[..., None]], axis=-1)
    sol = lax.linalg.triangular_solve(a, rhs, left_side=True, lower=True)
    u, w = sol[..., :DV], sol[..., DV:]
    attn = jnp.einsum('bhncd,bhnjd->bhncj', q, k) * decay
    q_dec = q * jnp.exp(gc)[..., None]
    g_last = gc[..., -1]
    k_dec = k * jnp.exp(g_last[..., None] - gc)[..., None]
    front = lambda t: jnp.moveaxis(t, 2, 0)
    xs = (front(q_dec), front(k_dec), front(u), front(w), front(attn), front(g_last))

    def step(state, inp):
        q_n, k_n, u_n, w_n, attn_n, gl = inp
        v_new = u_n - jnp.einsum('bhcd,bhde->bhce', w_n, state)
        o = jnp.einsum('bhcd,bhde->bhce', q_n, state) + jnp.einsum('bhcj,bhje->bhce', attn_n, v_new)
        state = state * jnp.exp(gl)[..., None, None] + jnp.einsum('bhcd,bhce->bhde', k_n, v_new)
        return state, o

    _, o = lax.scan(step, jnp.zeros((B, H, DK, DV), jnp.float32), xs)
    return o.transpose(1, 0, 3, 2, 4).reshape(B, S, H, DV)

def hybrid_layer(x, norm_g, w_in, conv_w, a_log, dt_bias, dn_g, w_up_r, w_up_d, w_o):
    B, S, _ = x.shape
    f32 = jnp.float32
    h = rmsnorm(x, norm_g)
    proj = h @ w_in
    (rq, rk, rv, rz, dq, dk, dv, dz, db, da, gr, gd) = jnp.split(proj, _split_points(), axis=-1)

    pos = jnp.arange(S)
    rq = rope(rq.reshape(B, S, RET_HEADS, RET_DK).astype(f32), pos)
    rk = rope(rk.reshape(B, S, RET_HEADS, RET_DK).astype(f32), pos) * (RET_DK ** -0.5)
    rv = rv.reshape(B, S, RET_HEADS, RET_DV).astype(f32)
    o_r = retention(rq, rk, rv)
    mu = jnp.mean(o_r, axis=-1, keepdims=True)
    var = jnp.mean(jnp.square(o_r - mu), axis=-1, keepdims=True)
    o_r = ((o_r - mu) * lax.rsqrt(var + EPS)).reshape(B, S, RET_V_W).astype(x.dtype)
    o_r = o_r * jax.nn.silu(rz)

    qkv = jax.nn.silu(causal_conv(jnp.concatenate([dq, dk, dv], axis=-1), conv_w))
    dq, dk, dv = jnp.split(qkv, [DN_QK_W, 2 * DN_QK_W], axis=-1)
    dq = l2norm(dq.reshape(B, S, DN_HEADS, DN_DK).astype(f32)) * (DN_DK ** -0.5)
    dk = l2norm(dk.reshape(B, S, DN_HEADS, DN_DK).astype(f32))
    dv = dv.reshape(B, S, DN_HEADS, DN_DV).astype(f32)
    beta = jax.nn.sigmoid(db.astype(f32))
    g = -jnp.exp(a_log.astype(f32)) * jax.nn.softplus(da.astype(f32) + dt_bias.astype(f32))
    o_d = gated_deltanet(dq, dk, dv, beta, g)
    o_d = o_d * lax.rsqrt(jnp.mean(o_d * o_d, axis=-1, keepdims=True) + EPS) * dn_g.astype(f32)
    o_d = o_d.reshape(B, S, DN_V_W).astype(x.dtype) * jax.nn.silu(dz)

    y = jax.nn.sigmoid(gr) * (o_r @ w_up_r) + jax.nn.sigmoid(gd) * (o_d @ w_up_d)
    return x + y @ w_o

def setup_inputs(seed: int = 0) -> dict:
    key = jax.random.key(seed)
    ks = jax.random.split(key, 12)
    f32 = jnp.float32
    x = jax.random.normal(ks[0], (BATCH, SEQ, D_MODEL), f32)
    norm_gain = 1.0 + 0.02 * jax.random.normal(ks[1], (DEPTH, D_MODEL), f32)
    w_in = jax.random.normal(ks[2], (DEPTH, D_MODEL, IN_W), f32) * D_MODEL ** -0.5
    conv_w = jax.random.normal(ks[3], (DEPTH, CONV_K, CONV_W), f32) * CONV_K ** -0.5
    a_log = jnp.log(jax.random.uniform(ks[4], (DEPTH, DN_HEADS), f32, 1.0, 16.0))
    dt = jnp.exp(jax.random.uniform(ks[5], (DEPTH, DN_HEADS), f32, np.log(1e-3), np.log(1e-1)))
    dt_bias = dt + jnp.log(-jnp.expm1(-dt))
    dn_norm_gain = 1.0 + 0.02 * jax.random.normal(ks[6], (DEPTH, DN_DV), f32)
    w_up_ret = jax.random.normal(ks[7], (DEPTH, RET_V_W, D_MODEL), f32) * RET_V_W ** -0.5
    w_up_dn = jax.random.normal(ks[8], (DEPTH, DN_V_W, D_MODEL), f32) * DN_V_W ** -0.5
    w_out = jax.random.normal(ks[9], (DEPTH, D_MODEL, D_MODEL), f32) * D_MODEL ** -0.5
    final_gain = 1.0 + 0.02 * jax.random.normal(ks[10], (D_MODEL,), f32)
    return {"x": x, "norm_gain": norm_gain, "w_in": w_in, "conv_w": conv_w, "a_log": a_log,
            "dt_bias": dt_bias, "dn_norm_gain": dn_norm_gain, "w_up_ret": w_up_ret,
            "w_up_dn": w_up_dn, "w_out": w_out, "final_gain": final_gain}

def reference(x, norm_gain, w_in, conv_w, a_log, dt_bias, dn_norm_gain, w_up_ret, w_up_dn,
              w_out, final_gain):
    for l in range(DEPTH):
        x = hybrid_layer(x, norm_gain[l], w_in[l], conv_w[l], a_log[l], dt_bias[l],
                         dn_norm_gain[l], w_up_ret[l], w_up_dn[l], w_out[l])
    return rmsnorm(x, final_gain)


_drawn_inputs = setup_inputs


def setup_inputs(seed=0):
    import zlib

    import numpy as np

    out = dict(_drawn_inputs(seed))
    spreads = {}
    factors = {'dn_norm_gain': 6.295, 'final_gain': 2.92}
    for name, (base, spread) in spreads.items():
        noise = np.random.default_rng([zlib.crc32(name.encode()), seed]).standard_normal(out[name].shape)
        drawn = base * np.exp(spread * noise) if base else spread * noise
        out[name] = __import__('jax').numpy.asarray(drawn.astype(out[name].dtype))
    for name, factor in factors.items():
        out[name] = (out[name] * factor).astype(out[name].dtype)
    return out
```

```python
from contextlib import ExitStack

import numpy as np
import concourse.bass as bass
from concourse import mybir

F32 = mybir.dt.float32
F32R = mybir.dt.float32r
ALU = mybir.AluOpType
ACT = mybir.ActivationFunctionType

P = 128
D_MODEL, SEQ, DEPTH = 1024, 1024, 2
KT = D_MODEL // P
HALF = 512
NHALF = SEQ // HALF
CPH = HALF // P
NCH = SEQ // P
RH, RDV = 4, 256
DH = 8
DK = 128
TAPS = 4
EPS = 1e-6
IN_W = 9232
RQ0, RK0, RV0, RZ0 = 0, 512, 1024, 2048
DQ0, DK0, DV0, DZ0 = 3072, 4096, 5120, 6144
BA0, GR0, GD0 = 7168, 7184, 8208
LEVELS = [2, 4, 8, 16, 32, 64]

BLK_BA, BLK_KVQ0, BLK_HEADS = 0, 2, 5
BLK_UPD = BLK_HEADS + 6 * DH - 3
BLK_RET = BLK_UPD + KT
BLK_UPR = BLK_RET + 6 * RH
BLK_OUT = BLK_UPR + KT
NBLK = BLK_OUT + KT

C_ID, C_UP, C_NEG, C_M1, C_LV, C_ONE = 0, P, 2 * P, 3 * P, 4 * P, 10 * P
C_ALL = 11 * P
ROW_CONV, ROW_NG, ROW_DN, ROW_FG = 0, 96, 104, 105
ROWS = 113
ARENA = 21056


class Signal:

    def __init__(self, handle, per):
        self.sem, self.per = handle, per

    def after(self, t, k):
        return t * self.per + (self.per + k)


def constants():
    i = np.arange(P)
    row, col = i[:, None], i[None, :]
    parts = [row == col, row <= col, np.where(col >= row, 0.0, -1e30), -1.0 * ((col == row + 1) & (row % 2 == 0))]
    for s in LEVELS:
        parts.append((row // (2 * s) == col // (2 * s)) & (row % (2 * s) >= s) & (col % (2 * s) < s))
    parts.append(np.ones((P, P)))
    masks = np.concatenate([np.asarray(p, np.float32) for p in parts], 1)
    half = DK // 2
    inv = np.power(np.float32(10000.0), -np.arange(half, dtype=np.float32) / np.float32(half)).astype(np.float32)
    ang = (np.arange(SEQ, dtype=np.float32)[:, None] * inv[None, :]).astype(np.float32).T
    cos, sin = np.cos(ang), np.sin(ang)
    rope = np.stack([np.concatenate([cos, cos]), np.concatenate([-sin, sin])], 1).astype(np.float32)
    ret = np.zeros((RH, P, 2 * P + 2), np.float64)
    for h in range(RH):
        lg = np.log1p(-(2.0 ** (-5 - h)))
        ret[h, :, 0:P] = np.where(col >= row, np.exp(np.maximum(col - row, 0) * lg), 0) * DK ** -0.5
        ret[h, :, P:2 * P] = np.exp((col + 1.0) * lg)
        ret[h, :, 2 * P] = np.exp((P - 1 - i) * lg) * DK ** -0.5
        ret[h, :, 2 * P + 1] = np.exp(P * lg)
    return {"masks": masks, "rope": rope.reshape(P, 2 * SEQ), "ret": ret.astype(np.float32)}


def deltanet_schedule(hf, fills):
    s = [("tokens",), 4, ("khat_back",), 2, ("grams",), 3, ("x_first",), 1]
    for n in range(len(LEVELS)):
        s += [("inv_y", n), 1, ("inv_xt", n), 2]
        if n < len(LEVELS) - 1:
            s += [("inv_x", n), 1 + n % 2]
    s += [("w",), 1]
    for c in range(CPH):
        s += [("v_new", c), 1, ("state_out", c), 1]
    s += [3, ("o_back",)]
    steps, left = [], fills
    for x in s:
        if isinstance(x, int):
            x = min(x, left)
            left -= x
            if x:
                steps.append(("fill", x))
        else:
            steps.append(x)
    if left:
        steps.insert(len(steps) - 1, ("fill", left))
    return steps


def build(nc, x, norm_gain, w_in, conv_w, a_log, dt_bias, dn_gain, w_up_ret, w_up_dn, w_out, final_gain,
          masks, rope, ret, out):
    ctx = ExitStack()
    with ctx:
        def sb(name, shape, dt=F32):
            return ctx.enter_context(nc.sbuf_tensor(name, shape, dt))

        def signal(name, per):
            s = Signal(ctx.enter_context(nc.semaphore(name)), per)
            signals.append(s)
            return s

        def plain(name):
            return ctx.enter_context(nc.semaphore(name))

        signals = []

        act_hi = sb("act_hi", [P, KT, SEQ], F32R)
        act_lo = sb("act_lo", [P, KT, SEQ], F32R)
        o_all = sb("o_all", [P, KT, SEQ])
        w_raw = sb("w_raw", [P, KT, P])
        w_hi = sb("w_hi", [P, 2, KT, P], F32R)
        w_lo = sb("w_lo", [P, 2, KT, P], F32R)
        mk = sb("mk", [P, C_ALL])
        cols = sb("cols", [P, P])
        small = sb("small", [P, 4, DH, NCH])
        g_tok = sb("g_tok", [P, NCH, DH])
        abias = sb("abias", [P, 3, DH])
        dngh = sb("dngh", [P, 1])
        negh = sb("negh", [P, 16])
        arena_at = -(-nc.sbuf_base // 32) * 32
        arena = sb("arena", [P, ARENA])
        ident, upper, ones = mk[:, C_ID:C_ID + P], mk[:, C_UP:C_UP + P], mk[:, C_ONE:C_ONE + P]

        def bcast4(ap):
            return ap.unsqueeze(1).to_broadcast([P, CPH, P])

        place = {"at": 0}

        def plan():
            place["at"] = 0

        def ar(name, shape, dt=F32):
            n = int(np.prod(shape[1:]))
            a = place["at"]
            place["at"] = a + n
            assert place["at"] <= ARENA, (name, place)
            if dt is F32:
                v = arena[:, a:a + n]
                if len(shape) == 3:
                    v = v.rearrange("p (a b) -> p a b", a=shape[1])
                if len(shape) == 4:
                    v = v.rearrange("p (a b c) -> p a b c", a=shape[1], b=shape[2])
                return v
            return nc.alloc_sbuf_tensor_at(name, shape, dt, offset=arena_at + 4 * a)

        plan()
        raw = ar("raw", [P, 2, SEQ + 4])
        acc = ar("acc", [P, 2, HALF])
        th = ar("th", [P, 2, HALF])
        kqv = ar("kqv", [P, 3, SEQ])
        sz = ar("sz", [P, SEQ])
        gate_t = ar("gate_t", [P, 2, HALF])
        sq = ar("sq", [P, 2, HALF])
        gcb = ar("gcb", [P, HALF])
        beb = ar("beb", [P, HALF])
        hs = ar("hs", [P, 4, NCH])
        nrm = ar("nrm", [P, 4, 8])
        kh, khT, kd, kw, vb = (ar(n, [P, CPH, P]) for n in ("kh", "khT", "kd", "kw", "vb"))
        dec, decb, egc, qd = (ar(n, [P, CPH, P]) for n in ("dec", "decb", "egc", "qd"))
        lT, aT, xT, xx, yy, nw = (ar(n, [P, CPH, P]) for n in ("lT", "aT", "xT", "xx", "yy", "nw"))
        t0 = ar("t0", [P, CPH, P])
        on = ar("on", [P, CPH, P])
        vn = ar("vn", [P, 2, P])
        state = ar("state", [P, 2, P])
        og = ar("og", [P, 6, CPH])
        plan()
        rope_t = ar("rope_t", [P, 2, SEQ])
        swap = ar("swap", [P, 2, HALF])
        rt1 = ar("rt1", [P, HALF])
        rt2 = ar("rt2", [P, HALF])
        rkq = ar("rkq", [P, 2, SEQ])
        rvT = ar("rvT", [P, 2, SEQ])
        rth = ar("rth", [P, 2, HALF])
        rsz = ar("rsz", [P, 2, SEQ])
        rcon = ar("rcon", [P, 2 * P + 2])
        rkd, rqd, rsc = (ar(n, [P, CPH, P]) for n in ("rkd", "rqd", "rsc"))
        rvt = ar("rvt", [P, CPH, RDV])
        ron = ar("ron", [P, CPH, RDV])
        rstate = ar("rstate", [P, 2, RDV])
        bst = ar("bst", [P, CPH, 6])
        bmv = ar("bmv", [P, CPH, 2])
        brs = ar("brs", [P, 2, CPH])
        plan()
        o_hi = ar("o_hi", [P, KT, SEQ], F32R)
        o_lo = ar("o_lo", [P, KT, SEQ], F32R)
        gy = ar("gy", [P, 2, HALF])
        y1 = ar("y1", [P, 2, HALF])
        yf = ar("yf", [P, 2, HALF])
        plan()
        nsq = ar("nsq", [P, 2, SEQ])
        ms = ar("ms", [P, SEQ])
        r0 = ar("r0", [P, SEQ])
        r1 = ar("r1", [P, SEQ])
        hfull = ar("hfull", [P, 2, SEQ])
        ba = arena[0:16, place["at"]:place["at"] + SEQ]
        place["at"] += SEQ
        btk = ar("btk", [P, NCH, 16])
        sp = ar("sp", [P, 4, NCH * DH])
        rows8 = arena[0:DH, place["at"]:place["at"] + 2 * SEQ].rearrange("p (a b) -> p a b", a=2)
        place["at"] += 2 * SEQ
        xin = ar("xin", [P, 2, D_MODEL])
        prow = arena[0:ROWS, place["at"]:place["at"] + P]

        dense_ps = ctx.enter_context(nc.psum_tensor("dense_ps", [P, 2, HALF], F32))
        wk = [ctx.enter_context(nc.psum_tensor(f"work{n}", [P, HALF], F32)) for n in range(6)]

        def chunks(bank):
            return wk[bank][:, :].rearrange("p (c t) -> p c t", c=CPH)

        x_dram = nc.dram_tensor("x_scratch", [KT, P, SEQ], F32)
        gate_dram = nc.dram_tensor("gate_scratch", [2, KT, P, SEQ], F32)
        y_dram = nc.dram_tensor("y_scratch", [KT, P, SEQ], F32)
        row_dram = nc.dram_tensor("row_scratch", [2, DH, SEQ], F32)

        const_in = plain("const_in")
        waited = plain("waited")
        prow_in = plain("prow_in")
        cols_ps, cols_ok = plain("cols_ps"), plain("cols_ok")
        xin_in = [plain("xin_in0"), plain("xin_in1")]
        xin_ps, xin_ok = plain("xin_ps"), plain("xin_ok")
        x0_stored = plain("x0_stored")
        out_ps, out_ok, out_stored = plain("out_ps"), plain("out_ok"), [plain("out_stored0"), plain("out_stored1")]
        pool_set = plain("pool_set")
        halo_ok = signal("halo_zeroed", 1)
        w_in_ok = signal("w_loaded", 16)
        w_hi_ok, w_lo_ok = signal("w_hi_ready", 1), signal("w_lo_ready", 1)
        dense_ok = [signal("dense_done0", 1), signal("dense_done1", 1)]
        dense_free = [signal("dense_free0", 1), signal("dense_free1", 1)]
        n_sq = signal("norm_squares", KT)
        n_ps = signal("norm_sums", KT)
        n_step = signal("norm_steps", 8)
        n_act = signal("norm_act", 2)
        n_full = signal("norm_scaled", KT)
        n_hi, n_lo = signal("norm_hi", KT), signal("norm_lo", KT)
        b_in = signal("abias_loaded", 32)
        b_row = signal("ba_rows", 2)
        b_tokps = signal("ba_tokens_psum", 1)
        b_dve, b_act = signal("ba_vector", 8), signal("ba_scalar", 8)
        b_gcps, b_rowps, b_rows = signal("gc_psum", 1), signal("rows_psum", 2), signal("rows_ready", 2)
        b_st = signal("rows_stored", 16)
        raw_ok = signal("raw_ready", 6)
        conv_s = signal("conv_steps", 24)
        th_ok = signal("tanh_ready", 8)
        kqv_ok = signal("kqv_ready", 6)
        sz_ok = signal("z_silu_ready", 2)
        gt_ok = signal("gate_tanh_ready", 4)
        gt_st = [signal("gate_stored0", 32), signal("gate_stored1", 32)]
        row_in = [signal("gc_row_loaded", 32), signal("beta_row_loaded", 32)]
        hs_ok = signal("head_scalars", 1)
        sq_ok = signal("squares_ready", 4)
        tok_ps = signal("tokens_psum", 2)
        nrm_s, nrm_p = signal("norms_ready", 2), signal("norm_power", 2)
        kh_ok, vb_ok = signal("khat_ready", 2), signal("vbeta_ready", 2)
        khb_ps, khT_ok = signal("khat_back_psum", 2), signal("khatT_ready", 2)
        kw_ok, kd_ok = signal("k_w_ready", 2), signal("k_dec_ready", 2)
        dif_ok, dec_ok, decb_ok = signal("gc_diff", 4), signal("decay_ready", 2), signal("decay_beta_ready", 2)
        egc_ok, qd_ok = signal("exp_gc_ready", 2), signal("q_dec_ready", 2)
        gram_ps = signal("grams_psum", 2)
        lT_ok, aT_ok, l1_ok = signal("lT_ready", 2), signal("attnT_ready", 2), signal("l1_ready", 2)
        xT_ok, x_ps, x_ok = signal("xT_ready", 14), signal("x_psum", 12), signal("x_ready", 12)
        y_ps, y_ok, xt_ps = signal("y_psum", 12), signal("y_ready", 12), signal("xt_psum", 12)
        w_ps, nw_ok = signal("w_psum", 2), signal("neg_w_ready", 2)
        vn_ps, vn_ok = signal("v_new_psum", 8), signal("v_new_ready", 8)
        st_ps, st_ok = signal("state_psum", 8), signal("state_ready", 8)
        o_ps = signal("o_psum", 8)
        osq_ok, og_s, og_p, on_ok = signal("o_squares", 2), signal("o_norm_steps", 8), signal("o_power", 2), signal("o_normed", 2)
        ob_ps, ob_ok = signal("o_back_psum", 2), signal("o_ready", 2)
        rgl = signal("o_scale", 2)
        rope_in = signal("rope_loaded", 16)
        rc_in = signal("ret_consts_loaded", 16)
        swap_ok = signal("swap_ready", 8)
        rrot, rpart = signal("rope_parts", 8), signal("rope_ready", 4)
        rv_ok, rth_ok, rsz_ok = signal("rv_ready", 4), signal("rz_tanh", 4), signal("rz_silu", 4)
        rtok_ps = signal("ret_tokens_psum", 4)
        rkd_ok, rvt_ok, rqd_ok = signal("ret_kdec", 2), signal("ret_vtok", 4), signal("ret_qdec", 2)
        rsc_ps, rsc_ok = signal("ret_scores_psum", 2), signal("ret_scores", 2)
        rkv_ps, rst_ok = signal("ret_kv_psum", 8), signal("ret_state", 8)
        ro_ps, rbn = signal("ret_o_psum", 8), signal("ret_stats", 20)
        rpw, ron_ok = signal("ret_rstd", 2), signal("ret_o_normed", 2)
        rob_ps, rob_ok = signal("ret_o_back_psum", 4), signal("ret_o_ready", 4)
        oh_ok, ol_ok = signal("o_hi_ready", 1), signal("o_lo_ready", 1)
        g_in = [signal("gate_loaded0", 16), signal("gate_loaded1", 16)]
        y_in = [signal("y_loaded0", 16), signal("y_loaded1", 16)]
        y_st = [signal("y_stored0", 16), signal("y_stored1", 16)]
        yg_ok, yf_ok = signal("y_gated", 2), signal("y_merged", 2)
        yh_ok, yl_ok = signal("y_hi", 2), signal("y_lo", 2)
        xo_in = [signal("x_loaded0", 16), signal("x_loaded1", 16)]
        xn_ok = signal("x_new", 2)
        xn_st = signal("x_stored", 32)

        def settled(eng):
            eng.sem_inc(waited, 1)

        block = ctx.enter_context(nc.Block())

        def w_src(t, what, col=0):
            return what[t, :, bass.ds(col, P)].rearrange("(k p) n -> p k n", p=P)

        @block.sync
        def _(eng):
            for s in signals:
                eng.sem_inc(s.sem, s.per)
            eng.dma_start(mk[:, :], masks).then_inc(const_in, 16)
            cw = conv_w

            def load_w(g, src, parts=1):
                eng.wait_ge(w_lo_ok.sem, w_lo_ok.after(g, 0))
                settled(eng)
                for a in range(parts):
                    ks = slice(a * KT // parts, (a + 1) * KT // parts)
                    eng.dma_start(w_raw[:, ks, :], src[:, ks, :]).then_inc(w_in_ok.sem, 16)

            for i in range(NCH):
                if i >= 2:
                    eng.wait_ge(xin_ps, i - 1)
                eng.dma_start(xin[:, i % 2, :], x[0, i * P:(i + 1) * P, :]).then_inc(xin_in[i % 2], 16)
            eng.wait_ge(xin_ok, 2 * NCH)
            eng.dma_start(x_dram[:, :, :].rearrange("k p t -> p k t"), o_all[:, :, :]).then_inc(x0_stored, 16)

            with eng.Fori(0, DEPTH) as lay:
                l = eng.snap(lay)
                n = eng.snap(lay * NBLK)
                eng.wait_ge(n_hi.sem, n_hi.after(l, 0))
                settled(eng)
                eng.wait_ge(xn_ok.sem, xn_ok.after(l * KT, 0))
                settled(eng)
                eng.dma_start(prow[ROW_CONV:ROW_CONV + 96, :],
                              cw[l].rearrange("k (b c) -> (k b) c", c=P)).then_inc(prow_in, 16)
                eng.dma_start(prow[ROW_NG:ROW_NG + KT, :],
                              norm_gain[l].rearrange("(k p) -> k p", p=P)).then_inc(prow_in, 16)
                eng.dma_start(prow[ROW_DN:ROW_DN + 1, :],
                              dn_gain[l].rearrange("(k p) -> k p", p=P)).then_inc(prow_in, 16)
                eng.dma_start(prow[ROW_FG:ROW_FG + KT, :],
                              final_gain.rearrange("(k p) -> k p", p=P)).then_inc(prow_in, 16)
                eng.dma_start(abias[:, 0, :], dt_bias[l].unsqueeze(0).to_broadcast([P, DH])).then_inc(b_in.sem, 16)
                eng.dma_start(abias[:, 1, :], a_log[l].unsqueeze(0).to_broadcast([P, DH])).then_inc(b_in.sem, 16)
                load_w(n + BLK_BA, w_src(l, w_in, BA0), 2)
                for j, c0 in enumerate((DK0, DV0, DQ0)):
                    load_w(n + BLK_KVQ0 + j, w_src(l, w_in, c0))
                eng.wait_ge(b_rows.sem, b_rows.after(l, 2))
                settled(eng)
                eng.dma_start(row_dram[:, :, :].rearrange("a h t -> h a t"), rows8).then_inc(b_st.sem, 16)
                eng.wait_ge(b_st.sem, b_st.after(l, 16))
                settled(eng)

                def head_loads(h, last):
                    t = eng.snap(l * DH + h)
                    m = eng.snap(n + h * 6)
                    rows = [row_dram[a, bass.ds(h, 1), :] for a in range(2)]
                    for hf in range(NHALF):
                        eng.wait_ge(egc_ok.sem, egc_ok.after(t, hf))
                        settled(eng)
                        eng.wait_ge(dif_ok.sem, dif_ok.after(t, 2 * hf))
                        settled(eng)
                        for a, dst in enumerate((gcb, beb)):
                            if a:
                                eng.wait_ge(decb_ok.sem, decb_ok.after(t, hf))
                                settled(eng)
                            eng.dma_start(dst, rows[a][:, hf * HALF:(hf + 1) * HALF].to_broadcast([P, HALF]))\
                               .then_inc(row_in[a].sem, 16)
                        if hf == 0:
                            for j, c0 in enumerate((DZ0, GD0, GR0)):
                                load_w(m + BLK_HEADS + j, w_src(l, w_in, c0 + h * P))
                        elif not last:
                            for j, c0 in enumerate((DK0, DV0, DQ0)):
                                load_w(m + BLK_HEADS + 3 + j, w_src(l, w_in, c0 + P + h * P))

                with eng.Fori(0, DH - 1) as h:
                    head_loads(h, False)
                head_loads(DH - 1, True)

                for j in range(KT):
                    load_w(n + (BLK_UPD + j), w_src(l, w_up_dn, j * P))
                with eng.Fori(0, RH) as h:
                    t = eng.snap(l * RH + h)
                    m = eng.snap(n + h * 6 + BLK_RET)
                    load_w(m, w_src(l, w_in, RK0 + h * P))
                    load_w(m + 1, w_src(l, w_in, RQ0 + h * P))
                    for j in range(2):
                        load_w(m + 2 + j, w_src(l, w_in, RV0 + j * P + h * RDV))
                    for j in range(2):
                        load_w(m + 4 + j, w_src(l, w_in, RZ0 + j * P + h * RDV))
                    eng.wait_ge(rst_ok.sem, rst_ok.after(t, 0))
                    settled(eng)
                    eng.wait_ge(rsc_ok.sem, rsc_ok.after(t, 0))
                    settled(eng)
                    eng.wait_ge(rqd_ok.sem, rqd_ok.after(t, 0))
                    settled(eng)
                    eng.dma_start(rcon, ret[bass.ds(h, 1), :, :].rearrange("h p n -> p (h n)")).then_inc(rc_in.sem, 16)

                for j in range(KT):
                    load_w(n + (BLK_UPR + j), w_src(l, w_up_ret, j * P))
                for j in range(KT):
                    load_w(n + (BLK_OUT + j), w_src(l, w_out, j * P))
                eng.wait_ge(xn_ok.sem, xn_ok.after(l * KT + KT - 1, 2))
                settled(eng)
                for c in range(2):
                    eng.dma_start(x_dram[4 * c:4 * c + 4, :, :].rearrange("k p t -> p k t"),
                                  o_all[:, 4 * c:4 * c + 4, :]).then_inc(xn_st.sem, 16)
            for i in range(NCH):
                eng.wait_ge(out_ok, 2 * i + 2)
                eng.dma_start(out[0, i * P:(i + 1) * P, :], xin[:, i % 2, :]).then_inc(out_stored[i % 2], 16)
            for s in out_stored:
                eng.wait_ge(s, 16 * NCH // 2)
            eng.wait_ge(xn_st.sem, xn_st.after(DEPTH - 1, 32))
            settled(eng)

        @block.tensor
        def _(eng):
            def turn(bank, blocks, cols_each=P):
                for c, src in enumerate(blocks):
                    mm = eng.transpose(wk[bank][:, c * P:(c + 1) * P], src, ident)
                return mm

            def dense_pieces(g, slot, hi, lo, inc=1, ready=None):
                for b in range(NHALF):
                    seg = slice(b * HALF, (b + 1) * HALF)
                    for k in range(KT):
                        if k == 0:
                            if b == 0:
                                eng.wait_ge(w_lo_ok.sem, w_lo_ok.after(g, 1))
                            eng.wait_ge(dense_free[b].sem, dense_free[b].after(g, 0))
                        if ready is not None and b == 0:
                            eng.wait_ge(*ready(k))
                        eng.matmul(dense_ps[:, b, :], w_hi[:, slot, k, :], hi[:, k, seg],
                                   start=(k == 0), stop=False)
                        eng.matmul(dense_ps[:, b, :], w_hi[:, slot, k, :], lo[:, k, seg],
                                   start=False, stop=False)
                        mm = eng.matmul(dense_ps[:, b, :], w_lo[:, slot, k, :], hi[:, k, seg],
                                        start=False, stop=(k == KT - 1))
                        if k == KT - 1:
                            mm.then_inc(dense_ok[b].sem, inc)
                        yield

            def dense(*a, **kw):
                for _ in dense_pieces(*a, **kw):
                    pass

            eng.wait_ge(const_in, 16)
            for i in range(NCH):
                eng.wait_ge(xin_in[i % 2], 16 * (i // 2 + 1))
                for a in range(2):
                    if i >= 1:
                        eng.wait_ge(xin_ok, 2 * i - 1 + a)
                    mm = turn(a, [xin[:, i % 2, (4 * a + c) * P:(4 * a + c + 1) * P] for c in range(4)])
                    if a == 1:
                        mm.then_inc(xin_ps, 1)
                    else:
                        mm.then_inc(out_ps, 1)

            def norm_sums(t):
                for k in range(KT):
                    eng.wait_ge(n_sq.sem, n_sq.after(t, k + 1))
                    for b in range(NHALF):
                        mm = eng.matmul(wk[b][:, :], ones, nsq[:, k % 2, b * HALF:(b + 1) * HALF],
                                        start=(k == 0), stop=(k == KT - 1))
                    mm.then_inc(n_ps.sem, 1)

            with eng.Fori(0, DEPTH) as lay:
                l = eng.snap(lay)
                n = eng.snap(lay * NBLK)
                eng.wait_ge(prow_in, l * 64 + 64)
                settled(eng)
                eng.transpose(wk[2][:, 0:ROWS], prow, ident[0:ROWS, 0:ROWS]).then_inc(cols_ps, 1)
                norm_sums(l)
                dense(n + BLK_BA, 0, act_hi, act_lo, 2, lambda k: (n_lo.sem, n_lo.after(l, k + 1)))

                eng.wait_ge(b_row.sem, b_row.after(l, 2))
                settled(eng)
                for c in range(NCH):
                    mm = eng.transpose(wk[3][:, 16 * c:16 * c + 16], ba[:, c * P:(c + 1) * P], ident[0:16, 0:16])
                mm.then_inc(b_tokps.sem, 1)
                dense(n + BLK_KVQ0, 0, act_hi, act_lo)
                eng.wait_ge(b_dve.sem, b_dve.after(l, 6))
                eng.matmul(wk[4][:, 0:64], upper, g_tok[:, :, :].rearrange("p c h -> p (c h)"), start=True, stop=True)
                eng.matmul(wk[4][:, 64:128], ones, g_tok[:, :, :].rearrange("p c h -> p (c h)"), start=True, stop=True)\
                   .then_inc(b_gcps.sem, 1)
                eng.wait_ge(b_act.sem, b_act.after(l, 7))
                for a in range(2):
                    for c in range(NCH):
                        if a and c == 0:
                            eng.wait_ge(b_rows.sem, b_rows.after(l, 1))
                        mm = eng.transpose(wk[c // 4][0:DH, (c % 4) * P:(c % 4 + 1) * P],
                                           small[:, 1 - a, :, c], ident)
                    mm.then_inc(b_rowps.sem, 1)
                for j in range(1, 3):
                    dense(n + BLK_KVQ0 + j, j % 2, act_hi, act_lo)

                def delta_head(h, last):
                    t = eng.snap(l * DH + h)
                    m = eng.snap(n + h * 6)

                    def stream(hf):
                        js = range(3) if hf == 0 else range(0 if last else 3)
                        for j in js:
                            jj = 3 * hf + j
                            yield from dense_pieces(m + BLK_HEADS + jj, (BLK_HEADS + jj) % 2, act_hi, act_lo)

                    for hf in range(NHALF):
                        fills = stream(hf)
                        seg = slice(hf * HALF, (hf + 1) * HALF)

                        def ch(ap, c):
                            return ap[:, hf * HALF + c * P:hf * HALF + (c + 1) * P]

                        for step in deltanet_schedule(hf, 16 * (3 if hf == 0 or not last else 0)):
                            what = step[0]
                            if what == "fill":
                                for _ in range(step[1]):
                                    next(fills)
                            elif what == "tokens":
                                eng.wait_ge(sq_ok.sem, sq_ok.after(t, 2 * hf + 2))
                                eng.wait_ge(ob_ok.sem, ob_ok.after(t, hf))
                                for a in range(2):
                                    for c in range(CPH):
                                        eng.matmul(wk[2][:, CPH * a + c:CPH * a + c + 1],
                                                   sq[:, a, c * P:(c + 1) * P], ones[:, 0:1], start=True, stop=True)
                                turn(0, [ch(kqv[:, 0, :], c) for c in range(CPH)])
                                turn(1, [ch(kqv[:, 2, :], c) for c in range(CPH)]).then_inc(tok_ps.sem, 1)
                            elif what == "khat_back":
                                eng.wait_ge(kh_ok.sem, kh_ok.after(t, hf + 1))
                                turn(3, [kh[:, c, :] for c in range(CPH)]).then_inc(khb_ps.sem, 1)
                            elif what == "grams":
                                eng.wait_ge(khT_ok.sem, khT_ok.after(t, hf + 1))
                                for c in range(CPH):
                                    eng.matmul(wk[4][:, c * P:(c + 1) * P], khT[:, c, :], khT[:, c, :],
                                               start=True, stop=True)
                                for c in range(CPH):
                                    mm = eng.matmul(wk[5][:, c * P:(c + 1) * P], khT[:, c, :],
                                                    ch(kqv[:, 1, :], c), start=True, stop=True)
                                mm.then_inc(gram_ps.sem, 1)
                            elif what in ("x_first", "inv_x"):
                                i = 0 if what == "x_first" else step[1] + 1
                                eng.wait_ge(xT_ok.sem, xT_ok.after(t, 7 * hf + i + 1))
                                turn(2, [xT[:, c, :] for c in range(CPH)]).then_inc(x_ps.sem, 1)
                            elif what == "inv_y":
                                i = step[1]
                                eng.wait_ge(x_ok.sem, x_ok.after(t, 6 * hf + i + 1))
                                for c in range(CPH):
                                    mm = eng.matmul(wk[0][:, c * P:(c + 1) * P], lT[:, c, :], xx[:, c, :],
                                                    start=True, stop=True)
                                mm.then_inc(y_ps.sem, 1)
                            elif what == "inv_xt":
                                i = step[1]
                                eng.wait_ge(y_ok.sem, y_ok.after(t, 6 * hf + i + 1))
                                for c in range(CPH):
                                    mm = eng.matmul(wk[1][:, c * P:(c + 1) * P], yy[:, c, :], xT[:, c, :],
                                                    start=True, stop=True)
                                mm.then_inc(xt_ps.sem, 1)
                            elif what == "w":
                                eng.wait_ge(xT_ok.sem, xT_ok.after(t, 7 * hf + 7))
                                eng.wait_ge(kw_ok.sem, kw_ok.after(t, hf + 1))
                                for c in range(CPH):
                                    mm = eng.matmul(wk[3][:, c * P:(c + 1) * P], kw[:, c, :], xT[:, c, :],
                                                    start=True, stop=True)
                                mm.then_inc(w_ps.sem, 1)
                            elif what == "v_new":
                                c = step[1]
                                cc = CPH * hf + c
                                bank = wk[4][:, (c % 2) * P:(c % 2 + 1) * P]
                                if c == 0:
                                    eng.wait_ge(nw_ok.sem, nw_ok.after(t, hf + 1))
                                    eng.wait_ge(aT_ok.sem, aT_ok.after(t, hf + 1))
                                eng.matmul(bank, xT[:, c, :], vb[:, c, :], start=True, stop=(cc == 0))
                                if cc:
                                    eng.wait_ge(st_ok.sem, st_ok.after(t, cc))
                                    mm = eng.matmul(bank, nw[:, c, :], state[:, cc % 2, :], start=False, stop=True)
                                else:
                                    mm = eng.matmul(bank, xT[:, c, :], vb[:, c, :], start=True, stop=True)
                                mm.then_inc(vn_ps.sem, 1)
                            elif what == "state_out":
                                c = step[1]
                                cc = CPH * hf + c
                                eng.wait_ge(vn_ok.sem, vn_ok.after(t, cc + 1))
                                if c == 0:
                                    eng.wait_ge(kd_ok.sem, kd_ok.after(t, hf + 1))
                                    eng.wait_ge(qd_ok.sem, qd_ok.after(t, hf + 1))
                                eng.matmul(wk[5][:, (c % 2) * P:(c % 2 + 1) * P], kd[:, c, :], vn[:, c % 2, :],
                                           start=True, stop=True).then_inc(st_ps.sem, 1)
                                dst = wk[1][:, c * P:(c + 1) * P]
                                if cc:
                                    eng.matmul(dst, qd[:, c, :], state[:, cc % 2, :], start=True, stop=False)
                                eng.matmul(dst, aT[:, c, :], vn[:, c % 2, :], start=(cc == 0), stop=True)\
                                   .then_inc(o_ps.sem, 1)
                            elif what == "o_back":
                                eng.wait_ge(on_ok.sem, on_ok.after(t, hf + 1))
                                turn(2, [on[:, c, :] for c in range(CPH)]).then_inc(ob_ps.sem, 1)
                        for _ in fills:
                            pass

                with eng.Fori(0, DH - 1) as h:
                    delta_head(h, False)
                delta_head(DH - 1, True)

                for j in range(KT):
                    dense(n + BLK_UPD + j, (BLK_UPD + j) % 2, o_hi, o_lo,
                          ready=(lambda k: (ol_ok.sem, ol_ok.after(l * (2 * KT) + k, 1))) if j == 0 else None)

                with eng.Fori(0, RH) as h:
                    t = eng.snap(l * RH + h)
                    m = eng.snap(n + h * 6)
                    for j in range(6):
                        dense(m + BLK_RET + j, (BLK_RET + j) % 2, act_hi, act_lo)
                    for hf in range(NHALF):
                        def ch(ap, c):
                            return ap[:, hf * HALF + c * P:hf * HALF + (c + 1) * P]
                        eng.wait_ge(rpart.sem, rpart.after(t, 4))
                        eng.wait_ge(rv_ok.sem, rv_ok.after(t, 4))
                        eng.wait_ge(rob_ok.sem, rob_ok.after(t, 2 * hf))
                        eng.wait_ge(ron_ok.sem, ron_ok.after(t, hf))
                        turn(0, [ch(rkq[:, 0, :], c) for c in range(CPH)]).then_inc(rtok_ps.sem, 1)
                        for c in range(CPH):
                            mm = eng.matmul(wk[1][:, c * P:(c + 1) * P], ch(rkq[:, 0, :], c), ch(rkq[:, 1, :], c),
                                            start=True, stop=True)
                        mm.then_inc(rsc_ps.sem, 1)
                        for e in range(2):
                            mm = turn(2 + e, [ch(rvT[:, e, :], c) for c in range(CPH)])
                        mm.then_inc(rtok_ps.sem, 1)
                        eng.wait_ge(rkd_ok.sem, rkd_ok.after(t, hf + 1))
                        eng.wait_ge(rvt_ok.sem, rvt_ok.after(t, 2 * hf + 2))
                        eng.wait_ge(rsc_ok.sem, rsc_ok.after(t, hf + 1))
                        eng.wait_ge(rqd_ok.sem, rqd_ok.after(t, hf + 1))
                        for c in range(CPH):
                            cc = CPH * hf + c
                            if c >= 2:
                                eng.wait_ge(rst_ok.sem, rst_ok.after(t, cc - 1))
                            eng.matmul(wk[(0, 5)[c % 2]][:, 0:RDV], rkd[:, c, :], rvt[:, c, :], start=True, stop=True)\
                               .then_inc(rkv_ps.sem, 1)
                            dst = wk[4 if c < 2 else 1][:, (c % 2) * RDV:(c % 2 + 1) * RDV]
                            eng.matmul(dst, rsc[:, c, :], rvt[:, c, :], start=True, stop=(cc == 0))
                            if cc:
                                eng.wait_ge(rst_ok.sem, rst_ok.after(t, cc))
                                mm = eng.matmul(dst, rqd[:, c, :], rstate[:, cc % 2, :], start=False, stop=True)
                            else:
                                mm = eng.matmul(dst, rsc[:, c, :], rvt[:, c, :], start=True, stop=True)
                            mm.then_inc(ro_ps.sem, 1)
                        eng.wait_ge(ron_ok.sem, ron_ok.after(t, hf + 1))
                        for e in range(2):
                            turn(2 + e, [ron[:, c, e * P:(e + 1) * P] for c in range(CPH)]).then_inc(rob_ps.sem, 1)

                for j in range(KT):
                    dense(n + BLK_UPR + j, (BLK_UPR + j) % 2, o_hi, o_lo,
                          ready=(lambda k: (ol_ok.sem, ol_ok.after(l * (2 * KT) + (KT + k), 1))) if j == 0 else None)
                for j in range(KT):
                    dense(n + BLK_OUT + j, (BLK_OUT + j) % 2, act_hi, act_lo,
                          ready=(lambda k: (yl_ok.sem, yl_ok.after(l * KT + k, 2))) if j == 0 else None)
            norm_sums(DEPTH)
            eng.wait_ge(n_full.sem, n_full.after(DEPTH, KT))
            for i in range(NCH):
                for a in range(2):
                    if i >= 1:
                        eng.wait_ge(out_ok, 2 * i - 1 + a)
                    for c in range(4):
                        mm = eng.transpose(wk[a][:, c * P:(c + 1) * P], o_all[:, 4 * a + c, i * P:(i + 1) * P], ident)
                    mm.then_inc(out_ps, 1)

        @block.scalar
        def _(eng):
            def norm_squares(t):
                for k in range(KT):
                    eng.wait_ge(xn_ok.sem, xn_ok.after(t * KT, 0))
                    eng.wait_ge(n_ps.sem, n_ps.after(t, k - 1))
                    eng.activation(nsq[:, k % 2, :], o_all[:, k, :], ACT.Square).then_inc(n_sq.sem, 1)
                eng.wait_ge(n_step.sem, n_step.after(t, 2))
                eng.activation(r0, ms, ACT.Ln).then_inc(n_act.sem, 1)
                eng.wait_ge(n_act.sem, n_act.after(t, 1))
                eng.activation(r1, r0, ACT.Exp, scale=-0.5).then_inc(n_act.sem, 1)

            eng.wait_ge(xin_ok, 2 * NCH)
            with eng.Fori(0, DEPTH) as lay:
                l = eng.snap(lay)
                n = eng.snap(lay * NBLK)
                norm_squares(l)
                for b in range(NHALF):
                    eng.wait_ge(dense_ok[b].sem, dense_ok[b].after(n + BLK_BA, 2))
                    eng.activation(ba[:, b * HALF:(b + 1) * HALF], dense_ps[0:16, b, :], ACT.Copy)\
                       .then_inc(b_row.sem, 1)
                    eng.wait_ge(b_row.sem, b_row.after(l, b + 1))
                    eng.sem_inc(dense_free[b].sem, 2)
                eng.wait_ge(b_in.sem, b_in.after(l, 32))
                eng.activation(abias[:, 2, :], abias[:, 1, :], ACT.Exp).then_inc(b_act.sem, 1)
                eng.wait_ge(b_dve.sem, b_dve.after(l, 2))
                eng.activation(sp[:, 1, :], sp[:, 0, :], ACT.Abs).then_inc(b_act.sem, 1)
                eng.wait_ge(b_act.sem, b_act.after(l, 2))
                eng.activation(sp[:, 2, :], sp[:, 1, :], ACT.Exp, scale=-1.0).then_inc(b_act.sem, 1)
                eng.wait_ge(b_act.sem, b_act.after(l, 3))
                eng.activation(sp[:, 1, :], sp[:, 2, :], ACT.Ln, bias=ones[:, 0:1]).then_inc(b_act.sem, 1)
                eng.activation(sp[:, 3, :].rearrange("p (h c) -> p h c", h=DH),
                               btk[:, :, 0:DH].rearrange("p c h -> p h c"), ACT.Tanh, scale=0.5).then_inc(b_act.sem, 1)
                eng.wait_ge(b_gcps.sem, b_gcps.after(l, 1))
                eng.activation(sp[:, 0, :].rearrange("p (h c) -> p h c", h=DH),
                               wk[4][:, 0:64].rearrange("p (c h) -> p h c", h=DH), ACT.Exp).then_inc(b_act.sem, 1)
                eng.activation(small[:, 1, :, :], wk[4][:, 0:64].rearrange("p (c h) -> p h c", h=DH), ACT.Copy)\
                   .then_inc(b_act.sem, 1)
                eng.wait_ge(b_dve.sem, b_dve.after(l, 8))
                eng.activation(small[:, 3, :, :], sp[:, 2, :].rearrange("p (h c) -> p h c", h=DH), ACT.Exp)\
                   .then_inc(b_act.sem, 1)

                def raw_evac(g, t, first, b, buf):
                    eng.wait_ge(dense_ok[b].sem, dense_ok[b].after(g, 1))
                    eng.wait_ge(conv_s.sem, conv_s.after(t, 8 if first == 4 else 0))
                    eng.activation(raw[:, buf, 3 + b * HALF:3 + (b + 1) * HALF], dense_ps[:, b, :], ACT.Copy)\
                       .then_inc(raw_ok.sem, 1)
                    eng.wait_ge(raw_ok.sem, raw_ok.after(t, first + b + 1))
                    eng.sem_inc(dense_free[b].sem, 1)

                def kqv_tanh(t, j, b):
                    i = 2 * j + b
                    eng.wait_ge(conv_s.sem, conv_s.after(t, 4 * (i + 1)))
                    eng.wait_ge(kqv_ok.sem, kqv_ok.after(t, i - 1))
                    eng.wait_ge(sz_ok.sem, sz_ok.after(t, 0))
                    eng.activation(th[:, b, :], acc[:, b, :], ACT.Tanh, scale=0.5).then_inc(th_ok.sem, 1)

                t0r = eng.snap(l * DH)
                for j, buf in ((0, 0), (1, 1), (2, 0)):
                    for b in range(NHALF):
                        raw_evac(n + BLK_KVQ0 + j, t0r, 2 * j, b, buf)
                        kqv_tanh(t0r, j, b)

                def delta_head(h, last):
                    t = eng.snap(l * DH + h)
                    m = eng.snap(n + h * 6)

                    def finish_half(hf, i):
                        j, b = i // 2, i % 2
                        g = m + (BLK_HEADS + 3 * hf + j)
                        if hf == 0:
                            eng.wait_ge(dense_ok[b].sem, dense_ok[b].after(g, 1))
                            if j == 0:
                                eng.wait_ge(sz_ok.sem, sz_ok.after(t, 0))
                                eng.wait_ge(kqv_ok.sem, kqv_ok.after(t, 6))
                                eng.activation(th[:, b, :], dense_ps[:, b, :], ACT.Tanh, scale=0.5)\
                                   .then_inc(th_ok.sem, 1)
                            else:
                                eng.wait_ge(gt_st[b].sem, gt_st[b].after(t, 16 * (j - 1)))
                                eng.activation(gate_t[:, b, :], dense_ps[:, b, :], ACT.Tanh, scale=0.5)\
                                   .then_inc(gt_ok.sem, 1)
                                eng.wait_ge(gt_ok.sem, gt_ok.after(t, 2 * (j - 1) + b + 1))
                                eng.sem_inc(dense_free[b].sem, 1)
                                eng.dma_start(gate_dram[j - 1, bass.ds(h, 1), :, b * HALF:(b + 1) * HALF]
                                              .rearrange("k p t -> p (k t)"), gate_t[:, b, :])\
                                   .then_inc(gt_st[b].sem, 16)
                        else:
                            raw_evac(g, t + 1, 2 * j, b, (0, 1, 0)[j])
                            kqv_tanh(t + 1, j, b)

                    for hf in range(NHALF):
                        seg = slice(hf * HALF, (hf + 1) * HALF)
                        pieces = 0
                        eng.wait_ge(kqv_ok.sem, kqv_ok.after(t, 6))
                        eng.wait_ge(tok_ps.sem, tok_ps.after(t, hf))
                        for a in range(2):
                            eng.activation(sq[:, a, :], kqv[:, a, seg], ACT.Square).then_inc(sq_ok.sem, 1)
                        for step in deltanet_schedule(hf, 16 * (3 if hf == 0 or not last else 0)):
                            what = step[0]
                            if what == "fill":
                                for i in range(pieces // KT, (pieces + step[1]) // KT):
                                    finish_half(hf, i)
                                pieces += step[1]
                            elif what == "tokens":
                                eng.wait_ge(row_in[0].sem, row_in[0].after(t, 16 * hf + 16))
                                eng.wait_ge(st_ok.sem, st_ok.after(t, CPH * hf))
                                eng.wait_ge(qd_ok.sem, qd_ok.after(t, hf))
                                eng.activation(egc.rearrange("p c t -> p (c t)"), gcb, ACT.Exp).then_inc(egc_ok.sem, 1)
                                eng.wait_ge(dif_ok.sem, dif_ok.after(t, 2 * hf + 2))
                                eng.wait_ge(aT_ok.sem, aT_ok.after(t, hf))
                                eng.activation(dec, t0, ACT.Exp).then_inc(dec_ok.sem, 1)
                            elif what == "khat_back":
                                eng.wait_ge(khb_ps.sem, khb_ps.after(t, hf + 1))
                                eng.activation(khT, chunks(3), ACT.Copy).then_inc(khT_ok.sem, 1)
                            elif what in ("x_first", "inv_x"):
                                i = 0 if what == "x_first" else step[1] + 1
                                eng.wait_ge(x_ps.sem, x_ps.after(t, 6 * hf + i + 1))
                                eng.activation(xx, chunks(2), ACT.Copy).then_inc(x_ok.sem, 1)
                            elif what == "w":
                                eng.wait_ge(w_ps.sem, w_ps.after(t, hf + 1))
                                eng.activation(nw, chunks(3), ACT.Copy, scale=-1.0).then_inc(nw_ok.sem, 1)
                            elif what == "state_out" and step[1] == CPH - 1:
                                eng.wait_ge(o_ps.sem, o_ps.after(t, CPH * hf + CPH))
                                eng.wait_ge(l1_ok.sem, l1_ok.after(t, hf + 1))
                                eng.activation(xx, chunks(1), ACT.Square).then_inc(osq_ok.sem, 1)

                with eng.Fori(0, DH - 1) as h:
                    delta_head(h, False)
                delta_head(DH - 1, True)

                def merge_streams(a):
                    if a == 0:
                        for b in range(NHALF):
                            eng.wait_ge(gt_st[b].sem, gt_st[b].after(l * DH + DH - 1, 32))
                        eng.wait_ge(ob_ok.sem, ob_ok.after(l * DH + DH - 1, 2))
                    else:
                        for b in range(NHALF):
                            eng.wait_ge(y_st[b].sem, y_st[b].after(l * KT + KT - 1, 16))
                        eng.wait_ge(rob_ok.sem, rob_ok.after(l * RH + RH - 1, 4))
                    for j in range(KT):
                        g = l * (2 * KT) + (a * KT + j)
                        for b in range(NHALF):
                            seg = slice(b * HALF, (b + 1) * HALF)
                            eng.wait_ge(yg_ok.sem, yg_ok.after(g, b - 1))
                            eng.dma_start(gy[:, b, :], gate_dram[a, j, :, seg]).then_inc(g_in[b].sem, 16)
                            if a:
                                eng.wait_ge(yf_ok.sem, yf_ok.after(l * KT + j, b - 1))
                                eng.dma_start(y1[:, b, :], y_dram[j, :, seg]).then_inc(y_in[b].sem, 16)
                        if a == 0:
                            for b in range(NHALF):
                                eng.wait_ge(yg_ok.sem, yg_ok.after(g, b + 1))
                                eng.dma_start(y_dram[j, :, b * HALF:(b + 1) * HALF], y1[:, b, :])\
                                   .then_inc(y_st[b].sem, 16)

                merge_streams(0)
                for b in range(NHALF):
                    eng.wait_ge(y_st[b].sem, y_st[b].after(l * KT + KT - 1, 16))
                eng.dma_start(rope_t, rope.rearrange("p (a t) -> p a t", a=2)).then_inc(rope_in.sem, 16)
                with eng.Fori(0, RH) as h:
                    t = eng.snap(l * RH + h)
                    m = eng.snap(n + h * 6)
                    for j in range(2):
                        for b in range(NHALF):
                            eng.wait_ge(dense_ok[b].sem, dense_ok[b].after(m + BLK_RET + j, 1))
                            eng.wait_ge(rrot.sem, rrot.after(t, 4 * j + 2 * b - 2))
                            for s in range(2):
                                eng.activation(swap[64 * s:64 * s + 64, b, :],
                                               dense_ps[64 - 64 * s:128 - 64 * s, b, :], ACT.Copy)\
                                   .then_inc(swap_ok.sem, 1)
                    for e in range(2):
                        for b in range(NHALF):
                            eng.wait_ge(dense_ok[b].sem, dense_ok[b].after(m + BLK_RET + 2 + e, 1))
                            eng.wait_ge(rtok_ps.sem, rtok_ps.after(t, 0))
                            eng.activation(rvT[:, e, b * HALF:(b + 1) * HALF], dense_ps[:, b, :], ACT.Copy)\
                               .then_inc(rv_ok.sem, 1)
                            eng.wait_ge(rv_ok.sem, rv_ok.after(t, 2 * e + b + 1))
                            eng.sem_inc(dense_free[b].sem, 1)
                    for e in range(2):
                        for b in range(NHALF):
                            eng.wait_ge(dense_ok[b].sem, dense_ok[b].after(m + BLK_RET + 4 + e, 1))
                            eng.wait_ge(rsz_ok.sem, rsz_ok.after(t, 2 * e + b - 1))
                            eng.activation(rth[:, b, :], dense_ps[:, b, :], ACT.Tanh, scale=0.5).then_inc(rth_ok.sem, 1)
                    for hf in range(NHALF):
                        eng.wait_ge(rtok_ps.sem, rtok_ps.after(t, 2 * hf + 2))
                        eng.wait_ge(ro_ps.sem, ro_ps.after(t, CPH * hf))
                        for e in range(2):
                            eng.activation(rvt[:, :, e * P:(e + 1) * P], chunks(2 + e), ACT.Copy).then_inc(rvt_ok.sem, 1)

                merge_streams(1)
                eng.wait_ge(yf_ok.sem, yf_ok.after(l * KT + KT - 1, 2))
                eng.wait_ge(x0_stored, 16)
                eng.wait_ge(xn_st.sem, xn_st.after(l, 0))
                for j in range(KT):
                    for b in range(NHALF):
                        eng.wait_ge(xn_ok.sem, xn_ok.after(l * KT + j, b - 1))
                        eng.dma_start(y1[:, b, :], x_dram[j, :, b * HALF:(b + 1) * HALF]).then_inc(xo_in[b].sem, 16)
            norm_squares(DEPTH)
            for i in range(NCH):
                eng.wait_ge(out_ps, NCH + 2 * i + 1)
                if i >= 2:
                    eng.wait_ge(out_stored[i % 2], 16 * (i // 2))
                eng.activation(xin[:, i % 2, 0:HALF], wk[0][:, :], ACT.Copy).then_inc(out_ok, 1)
                eng.wait_ge(out_ps, NCH + 2 * i + 2)
                eng.wait_ge(out_ok, 2 * i + 1)
                eng.activation(xin[:, i % 2, HALF:SEQ], wk[1][:, :], ACT.Copy).then_inc(out_ok, 1)

        @block.vector
        def _(eng):
            def split_w(g, slot, inc=1):
                eng.wait_ge(w_in_ok.sem, w_in_ok.after(g, 16 * inc))
                eng.wait_ge(dense_ok[1].sem, dense_ok[1].after(g, -1))
                eng.tensor_copy(w_hi[:, slot, :, :], w_raw[:, :, :]).then_inc(w_hi_ok.sem, inc)

            def norm_apply(t, final):
                for b in range(NHALF):
                    eng.wait_ge(n_ps.sem, n_ps.after(t, KT))
                    eng.tensor_scalar(ms[:, b * HALF:(b + 1) * HALF], wk[b][:, :], 1.0 / D_MODEL, EPS,
                                      ALU.mult, ALU.add).then_inc(n_step.sem, 1)
                eng.wait_ge(n_act.sem, n_act.after(t, 2))
                eng.tensor_tensor(r0, r1, r1, ALU.mult).then_inc(n_step.sem, 1)
                eng.wait_ge(n_step.sem, n_step.after(t, 3))
                eng.tensor_tensor(r0, r0, ms, ALU.mult).then_inc(n_step.sem, 1)
                eng.wait_ge(n_step.sem, n_step.after(t, 4))
                eng.tensor_scalar(r0, r0, -0.5, 1.5, ALU.mult, ALU.add).then_inc(n_step.sem, 1)
                eng.wait_ge(n_step.sem, n_step.after(t, 5))
                eng.tensor_tensor(r1, r1, r0, ALU.mult).then_inc(n_step.sem, 3)
                eng.wait_ge(n_step.sem, n_step.after(t, 8))
                for k in range(KT):
                    gain = cols[:, (ROW_FG if final else ROW_NG) + k:(ROW_FG if final else ROW_NG) + k + 1]
                    if final:
                        eng.scalar_tensor_tensor(out=o_all[:, k, :], in0=o_all[:, k, :], scalar=gain, in1=r1,
                                                 op0=ALU.mult, op1=ALU.mult).then_inc(n_full.sem, 1)
                        continue
                    eng.wait_ge(n_lo.sem, n_lo.after(t, k - 1))
                    eng.scalar_tensor_tensor(out=hfull[:, k % 2, :], in0=o_all[:, k, :], scalar=gain, in1=r1,
                                             op0=ALU.mult, op1=ALU.mult).then_inc(n_full.sem, 1)
                    eng.wait_ge(n_full.sem, n_full.after(t, k + 1))
                    eng.tensor_copy(act_hi[:, k, :], hfull[:, k % 2, :]).then_inc(n_hi.sem, 1)

            for i in range(NCH):
                for a in range(2):
                    eng.wait_ge(*((out_ps, i + 1) if a == 0 else (xin_ps, i + 1)))
                    eng.tensor_copy(o_all[:, 4 * a:4 * a + 4, i * P:(i + 1) * P], chunks(a)).then_inc(xin_ok, 1)

            with eng.Fori(0, DEPTH) as lay:
                l = eng.snap(lay)
                n = eng.snap(lay * NBLK)
                eng.wait_ge(cols_ps, l + 1)
                eng.tensor_copy(cols[:, 0:ROWS], wk[2][:, 0:ROWS]).then_inc(cols_ok, 1)
                eng.wait_ge(cols_ok, l * 2 + 1)
                eng.tensor_scalar(dngh[:, :], cols[:, ROW_DN:ROW_DN + 1], 0.5, None, ALU.mult).then_inc(cols_ok, 1)
                split_w(n + BLK_BA, 0, 2)
                norm_apply(l, False)
                eng.wait_ge(n_lo.sem, n_lo.after(l, KT))
                eng.memset(raw[:, :, 0:3], 0.0).then_inc(halo_ok.sem, 1)
                split_w(n + BLK_KVQ0, 0)
                eng.wait_ge(b_tokps.sem, b_tokps.after(l, 1))
                eng.tensor_copy(btk, wk[3][:, 0:P].rearrange("p (c n) -> p c n", c=NCH)).then_inc(b_dve.sem, 1)
                eng.wait_ge(b_dve.sem, b_dve.after(l, 1))
                eng.wait_ge(b_in.sem, b_in.after(l, 32))
                split_w(n + BLK_KVQ0 + 1, 1)
                z3 = sp[:, 0, :].rearrange("p (c h) -> p c h", h=DH)
                eng.tensor_tensor(z3, btk[:, :, DH:16], abias[:, 0, :].unsqueeze(1).to_broadcast([P, NCH, DH]), ALU.add)\
                   .then_inc(b_dve.sem, 1)
                eng.wait_ge(b_act.sem, b_act.after(l, 4))
                eng.scalar_tensor_tensor(out=sp[:, 2, :], in0=sp[:, 0, :], scalar=0.0, in1=sp[:, 1, :],
                                         op0=ALU.max, op1=ALU.add).then_inc(b_dve.sem, 1)
                eng.wait_ge(b_dve.sem, b_dve.after(l, 3))
                eng.scalar_tensor_tensor(out=g_tok[:, :, :], in0=sp[:, 2, :].rearrange("p (c h) -> p c h", h=DH),
                                         scalar=-1.0, in1=abias[:, 2, :].unsqueeze(1).to_broadcast([P, NCH, DH]),
                                         op0=ALU.mult, op1=ALU.mult).then_inc(b_dve.sem, 1)
                eng.wait_ge(b_act.sem, b_act.after(l, 5))
                eng.tensor_scalar(small[:, 0, :, :], sp[:, 3, :].rearrange("p (h c) -> p h c", h=DH), 0.5, 0.5,
                                  ALU.mult, ALU.add).then_inc(b_dve.sem, 2)
                eng.wait_ge(b_act.sem, b_act.after(l, 7))
                eng.wait_ge(b_dve.sem, b_dve.after(l, 6))
                eng.tensor_tensor(small[:, 2, :, :], small[:, 0, :, :],
                                  sp[:, 0, :].rearrange("p (h c) -> p h c", h=DH), ALU.mult).then_inc(b_dve.sem, 1)
                eng.tensor_tensor(sp[:, 2, :].rearrange("p (h c) -> p h c", h=DH),
                                  wk[4][:, 64:128].rearrange("p (c h) -> p h c", h=DH), small[:, 1, :, :],
                                  ALU.subtract).then_inc(b_dve.sem, 1)
                for a in range(2):
                    eng.wait_ge(b_rowps.sem, b_rowps.after(l, a + 1))
                    eng.tensor_copy(rows8[:, a, 0:HALF], wk[0][0:DH, :])
                    eng.tensor_copy(rows8[:, a, HALF:SEQ], wk[1][0:DH, :]).then_inc(b_rows.sem, 1)

                def conv(t, h, j, b, buf):
                    i = 2 * j + b
                    which = (1, 2, 0)[j]
                    slot = (0, 2, 1)[j]
                    eng.wait_ge(raw_ok.sem, raw_ok.after(t, i + 1))
                    eng.wait_ge(kqv_ok.sem, kqv_ok.after(t, i - 1))
                    for k in range(TAPS):
                        src = raw[:, buf, k + b * HALF:k + (b + 1) * HALF]
                        wcol = cols[:, bass.ds(ROW_CONV + 24 * k + 8 * which + h, 1)]
                        if k == 0:
                            eng.tensor_scalar(acc[:, b, :], src, wcol, None, ALU.mult).then_inc(conv_s.sem, 1)
                        else:
                            eng.wait_ge(conv_s.sem, conv_s.after(t, 4 * i + k))
                            eng.scalar_tensor_tensor(out=acc[:, b, :], in0=src, scalar=wcol, in1=acc[:, b, :],
                                                     op0=ALU.mult, op1=ALU.add).then_inc(conv_s.sem, 1)

                def silu(t, j, b):
                    i = 2 * j + b
                    slot = (0, 2, 1)[j]
                    eng.wait_ge(th_ok.sem, th_ok.after(t, i + 1))
                    if j != 2:
                        eng.wait_ge(tok_ps.sem, tok_ps.after(t, 0))
                    else:
                        eng.wait_ge(gram_ps.sem, gram_ps.after(t, 0))
                        eng.wait_ge(qd_ok.sem, qd_ok.after(t, 0))
                    eng.wait_ge(sq_ok.sem, sq_ok.after(t, 0))
                    eng.scalar_tensor_tensor(out=kqv[:, slot, b * HALF:(b + 1) * HALF], in0=th[:, b, :], scalar=1.0,
                                             in1=acc[:, b, :], op0=ALU.add, op1=ALU.mult).then_inc(kqv_ok.sem, 1)

                t0r = eng.snap(l * DH)
                for j, buf in ((0, 0), (1, 1), (2, 0)):
                    for b in range(NHALF):
                        if b == 0 and j < 2:
                            split_w(n + BLK_KVQ0 + j + 2, j % 2)
                        conv(t0r, 0, j, b, buf)
                        silu(t0r, j, b)

                def delta_head(h, last):
                    t = eng.snap(l * DH + h)
                    m = eng.snap(n + h * 6)
                    eng.wait_ge(b_act.sem, b_act.after(l, 8))
                    eng.wait_ge(kw_ok.sem, kw_ok.after(t, 0))
                    eng.wait_ge(kd_ok.sem, kd_ok.after(t, 0))
                    eng.tensor_copy(hs, small[:, :, bass.ds(h, 1), :].rearrange("p a h c -> p a (h c)"))\
                       .then_inc(hs_ok.sem, 1)

                    def finish_half(hf, i):
                        j, b = i // 2, i % 2
                        idx = BLK_HEADS + 3 * hf + j
                        if b == 0:
                            split_w(m + idx + 1, (idx + 1) % 2)
                        if hf == 0:
                            if j == 0:
                                eng.wait_ge(th_ok.sem, th_ok.after(t, 6 + b + 1))
                                eng.wait_ge(ob_ok.sem, ob_ok.after(t, 0))
                                eng.scalar_tensor_tensor(out=sz[:, b * HALF:(b + 1) * HALF], in0=th[:, b, :],
                                                         scalar=1.0, in1=dense_ps[:, b, :], op0=ALU.add,
                                                         op1=ALU.mult).then_inc(sz_ok.sem, 1)
                                eng.wait_ge(sz_ok.sem, sz_ok.after(t, b + 1))
                                eng.sem_inc(dense_free[b].sem, 1)
                        else:
                            conv(t + 1, h + 1, j, b, (0, 1, 0)[j])
                            silu(t + 1, j, b)

                    for hf in range(NHALF):
                        cs = slice(CPH * hf, CPH * hf + CPH)
                        pieces = 0

                        def per_token(ap):
                            return ap.unsqueeze(2).to_broadcast([P, CPH, P])

                        for step in deltanet_schedule(hf, 16 * (3 if hf == 0 or not last else 0)):
                            what = step[0]
                            if what == "fill":
                                for i in range(pieces // KT, (pieces + step[1]) // KT):
                                    finish_half(hf, i)
                                pieces += step[1]
                            elif what == "tokens":
                                eng.wait_ge(tok_ps.sem, tok_ps.after(t, hf + 1))
                                eng.tensor_scalar(nrm[:, 0, :], wk[2][:, 0:8], 0.25, EPS, ALU.mult, ALU.add)\
                                   .then_inc(nrm_s.sem, 1)
                                if hf == 0:
                                    eng.wait_ge(hs_ok.sem, hs_ok.after(t, 1))
                                eng.scalar_tensor_tensor(out=vb, in0=chunks(1), scalar=0.5,
                                                         in1=per_token(hs[:, 0, cs]), op0=ALU.mult, op1=ALU.mult)\
                                   .then_inc(vb_ok.sem, 1)
                                eng.wait_ge(nrm_p.sem, nrm_p.after(t, hf + 1))
                                eng.scalar_tensor_tensor(out=kh, in0=chunks(0), scalar=0.5,
                                                         in1=per_token(nrm[:, 1, 0:CPH]), op0=ALU.mult, op1=ALU.mult)\
                                   .then_inc(kh_ok.sem, 1)
                            elif what == "grams":
                                eng.wait_ge(gram_ps.sem, gram_ps.after(t, hf + 1))
                                eng.wait_ge(decb_ok.sem, decb_ok.after(t, hf + 1))
                                eng.tensor_tensor(lT, chunks(4), decb, ALU.mult).then_inc(lT_ok.sem, 1)
                                eng.wait_ge(lT_ok.sem, lT_ok.after(t, hf + 1))
                                eng.tensor_tensor(t0, lT, bcast4(mk[:, C_M1:C_M1 + P]), ALU.mult).then_inc(l1_ok.sem, 1)
                                eng.wait_ge(l1_ok.sem, l1_ok.after(t, hf + 1))
                                eng.tensor_tensor(xT, t0, bcast4(ident), ALU.add).then_inc(xT_ok.sem, 1)
                                eng.tensor_tensor(aT, chunks(5), dec, ALU.mult).then_inc(aT_ok.sem, 1)
                            elif what == "inv_y":
                                i = step[1]
                                eng.wait_ge(y_ps.sem, y_ps.after(t, 6 * hf + i + 1))
                                eng.tensor_tensor(yy, chunks(0), bcast4(mk[:, C_LV + i * P:C_LV + (i + 1) * P]),
                                                  ALU.mult).then_inc(y_ok.sem, 1)
                            elif what == "inv_xt":
                                i = step[1]
                                eng.wait_ge(xt_ps.sem, xt_ps.after(t, 6 * hf + i + 1))
                                eng.tensor_tensor(xT, xT, chunks(1), ALU.subtract).then_inc(xT_ok.sem, 1)
                            elif what == "v_new":
                                c = step[1]
                                cc = CPH * hf + c
                                eng.wait_ge(vn_ps.sem, vn_ps.after(t, cc + 1))
                                eng.tensor_copy(vn[:, c % 2, :], wk[4][:, (c % 2) * P:(c % 2 + 1) * P])\
                                   .then_inc(vn_ok.sem, 1)
                            elif what == "state_out":
                                c = step[1]
                                cc = CPH * hf + c
                                eng.wait_ge(st_ps.sem, st_ps.after(t, cc + 1))
                                src = wk[5][:, (c % 2) * P:(c % 2 + 1) * P]
                                if cc == 0:
                                    eng.tensor_copy(state[:, 1, :], src).then_inc(st_ok.sem, 1)
                                else:
                                    eng.wait_ge(o_ps.sem, o_ps.after(t, cc))
                                    eng.wait_ge(st_ok.sem, st_ok.after(t, cc))
                                    eng.scalar_tensor_tensor(out=state[:, (cc + 1) % 2, :], in0=state[:, cc % 2, :],
                                                             scalar=egc[:, c, P - 1:P], in1=src, op0=ALU.mult,
                                                             op1=ALU.add).then_inc(st_ok.sem, 1)
                                if c == CPH - 1:
                                    k = 4 * hf
                                    pq = nrm[:, 1, CPH:8]
                                    eng.wait_ge(osq_ok.sem, osq_ok.after(t, hf + 1))
                                    eng.tensor_reduce(og[:, 0, :], xx, mybir.AxisListType.X, ALU.add).then_inc(og_s.sem, 1)
                                    eng.tensor_tensor(og[:, 1, :], pq, pq, ALU.mult).then_inc(og_s.sem, 1)
                                    eng.wait_ge(og_s.sem, og_s.after(t, k + 2))
                                    eng.tensor_tensor(og[:, 2, :], og[:, 0, :], og[:, 1, :], ALU.mult).then_inc(og_s.sem, 1)
                                    eng.wait_ge(og_s.sem, og_s.after(t, k + 3))
                                    eng.tensor_scalar(og[:, 3, :], og[:, 2, :], 0.25 / (DK * DK), EPS, ALU.mult, ALU.add)\
                                       .then_inc(og_s.sem, 1)
                                    eng.wait_ge(og_p.sem, og_p.after(t, hf + 1))
                                    eng.scalar_tensor_tensor(out=og[:, 5, :], in0=og[:, 4, :], scalar=0.5 * DK ** -0.5,
                                                             in1=pq, op0=ALU.mult, op1=ALU.mult).then_inc(rgl.sem, 1)
                                    eng.wait_ge(rgl.sem, rgl.after(t, hf + 1))
                                    eng.tensor_tensor(on, chunks(1), per_token(og[:, 5, :]), ALU.mult)\
                                       .then_inc(on_ok.sem, 1)
                            elif what == "o_back":
                                eng.wait_ge(ob_ps.sem, ob_ps.after(t, hf + 1))
                                eng.scalar_tensor_tensor(
                                    out=o_all[:, bass.ds(h, 1), hf * HALF:(hf + 1) * HALF].rearrange("p k t -> p (k t)"),
                                    in0=wk[2][:, :], scalar=dngh[:, 0:1], in1=sz[:, hf * HALF:(hf + 1) * HALF],
                                    op0=ALU.mult, op1=ALU.mult).then_inc(ob_ok.sem, 1)

                with eng.Fori(0, DH - 1) as h:
                    delta_head(h, False)
                delta_head(DH - 1, True)

                def merge(a):
                    for k in range(KT):
                        if k == 0:
                            if a == 0:
                                eng.wait_ge(ob_ok.sem, ob_ok.after(l * DH + DH - 1, 2))
                                for b in range(NHALF):
                                    eng.wait_ge(gt_st[b].sem, gt_st[b].after(l * DH + DH - 1, 32))
                            else:
                                eng.wait_ge(rob_ok.sem, rob_ok.after(l * RH + RH - 1, 4))
                        eng.tensor_copy(o_hi[:, k, :], o_all[:, k, :]).then_inc(oh_ok.sem, 1)
                    for j in range(KT):
                        idx = (BLK_UPR if a else BLK_UPD) + j
                        split_w(n + idx + 1, (idx + 1) % 2)
                        g = l * (2 * KT) + (a * KT + j)
                        for b in range(NHALF):
                            eng.wait_ge(dense_ok[b].sem, dense_ok[b].after(n + idx, 1))
                            eng.wait_ge(g_in[b].sem, g_in[b].after(g, 16))
                            if a == 0:
                                eng.wait_ge(y_st[b].sem, y_st[b].after(l * KT + j, 0))
                                eng.scalar_tensor_tensor(out=y1[:, b, :], in0=gy[:, b, :], scalar=1.0,
                                                         in1=dense_ps[:, b, :], op0=ALU.add, op1=ALU.mult)\
                                   .then_inc(yg_ok.sem, 1)
                                eng.wait_ge(yg_ok.sem, yg_ok.after(g, b + 1))
                                eng.sem_inc(dense_free[b].sem, 1)
                            else:
                                eng.wait_ge(yl_ok.sem, yl_ok.after(l * KT + j, b - 1))
                                eng.scalar_tensor_tensor(out=yf[:, b, :], in0=gy[:, b, :], scalar=1.0,
                                                         in1=dense_ps[:, b, :], op0=ALU.add, op1=ALU.mult)\
                                   .then_inc(yg_ok.sem, 1)
                                eng.wait_ge(yg_ok.sem, yg_ok.after(g, b + 1))
                                eng.sem_inc(dense_free[b].sem, 1)
                                eng.wait_ge(y_in[b].sem, y_in[b].after(l * KT + j, 16))
                                eng.tensor_tensor(yf[:, b, :], yf[:, b, :], y1[:, b, :], ALU.add).then_inc(yf_ok.sem, 1)
                                eng.wait_ge(yf_ok.sem, yf_ok.after(l * KT + j, b + 1))
                                eng.tensor_copy(act_hi[:, j, b * HALF:(b + 1) * HALF], yf[:, b, :]).then_inc(yh_ok.sem, 1)

                merge(0)

                with eng.Fori(0, RH) as h:
                    t = eng.snap(l * RH + h)
                    m = eng.snap(n + h * 6)
                    eng.wait_ge(rope_in.sem, rope_in.after(l, 16))
                    for j in range(2):
                        split_w(m + BLK_RET + j + 1, (BLK_RET + j + 1) % 2)
                        for b in range(NHALF):
                            i = 2 * j + b
                            seg = slice(b * HALF, (b + 1) * HALF)
                            eng.wait_ge(swap_ok.sem, swap_ok.after(t, 2 * i + 2))
                            eng.wait_ge(rpart.sem, rpart.after(t, i))
                            eng.tensor_tensor(rt1, dense_ps[:, b, :], rope_t[:, 0, seg], ALU.mult).then_inc(rrot.sem, 1)
                            eng.tensor_tensor(rt2, swap[:, b, :], rope_t[:, 1, seg], ALU.mult).then_inc(rrot.sem, 1)
                            eng.wait_ge(rrot.sem, rrot.after(t, 2 * i + 2))
                            eng.sem_inc(dense_free[b].sem, 1)
                            eng.tensor_tensor(rkq[:, j, seg], rt1, rt2, ALU.add).then_inc(rpart.sem, 1)
                    split_w(m + BLK_RET + 3, (BLK_RET + 3) % 2)
                    split_w(m + BLK_RET + 4, (BLK_RET + 4) % 2)
                    for e in range(2):
                        split_w(m + BLK_RET + 5 + e, (BLK_RET + 5 + e) % 2)
                        for b in range(NHALF):
                            eng.wait_ge(rth_ok.sem, rth_ok.after(t, 2 * e + b + 1))
                            eng.scalar_tensor_tensor(out=rsz[:, e, b * HALF:(b + 1) * HALF], in0=rth[:, b, :],
                                                     scalar=1.0, in1=dense_ps[:, b, :], op0=ALU.add, op1=ALU.mult)\
                               .then_inc(rsz_ok.sem, 1)
                            eng.wait_ge(rsz_ok.sem, rsz_ok.after(t, 2 * e + b + 1))
                            eng.sem_inc(dense_free[b].sem, 1)
                    for hf in range(NHALF):
                        seg = slice(hf * HALF, (hf + 1) * HALF)
                        eng.wait_ge(rc_in.sem, rc_in.after(t, 16))
                        eng.wait_ge(ro_ps.sem, ro_ps.after(t, CPH * hf))
                        eng.wait_ge(rpart.sem, rpart.after(t, 4))
                        eng.tensor_tensor(rqd, rkq[:, 1, seg].rearrange("p (c t) -> p c t", c=CPH),
                                          bcast4(rcon[:, P:2 * P]), ALU.mult).then_inc(rqd_ok.sem, 1)
                        eng.wait_ge(rtok_ps.sem, rtok_ps.after(t, 2 * hf + 1))
                        eng.tensor_scalar(rkd, chunks(0), rcon[:, 2 * P:2 * P + 1], None, ALU.mult)\
                           .then_inc(rkd_ok.sem, 1)
                        eng.wait_ge(rsc_ps.sem, rsc_ps.after(t, hf + 1))
                        eng.tensor_tensor(rsc, chunks(1), bcast4(rcon[:, 0:P]), ALU.mult).then_inc(rsc_ok.sem, 1)
                        for c in range(CPH):
                            cc = CPH * hf + c
                            eng.wait_ge(rkv_ps.sem, rkv_ps.after(t, cc + 1))
                            src = wk[(0, 5)[c % 2]][:, 0:RDV]
                            if cc == 0:
                                eng.tensor_copy(rstate[:, 1, :], src).then_inc(rst_ok.sem, 1)
                            else:
                                eng.wait_ge(ro_ps.sem, ro_ps.after(t, cc))
                                eng.wait_ge(rst_ok.sem, rst_ok.after(t, cc))
                                eng.scalar_tensor_tensor(out=rstate[:, (cc + 1) % 2, :], in0=rstate[:, cc % 2, :],
                                                         scalar=rcon[:, 2 * P + 1:2 * P + 2], in1=src,
                                                         op0=ALU.mult, op1=ALU.add).then_inc(rst_ok.sem, 1)
                        for c in range(CPH):
                            o_src = wk[4 if c < 2 else 1][:, (c % 2) * RDV:(c % 2 + 1) * RDV]
                            eng.wait_ge(ro_ps.sem, ro_ps.after(t, CPH * hf + 2 * (c // 2) + 2))
                            eng.bn_stats(bst[:, c, :], o_src).then_inc(rbn.sem, 1)
                        for c in range(CPH):
                            eng.wait_ge(rbn.sem, rbn.after(t, 10 * hf + c + 1))
                            settled(eng)
                            eng.bn_aggr(bmv[:, c, :], bst[:, c, :]).then_inc(rbn.sem, 1)
                        eng.wait_ge(rbn.sem, rbn.after(t, 10 * hf + 8))
                        eng.tensor_scalar(brs[:, 0, :], bmv[:, :, 1], EPS, None, ALU.add).then_inc(rbn.sem, 2)
                        eng.wait_ge(rpw.sem, rpw.after(t, hf + 1))
                        for c in range(CPH):
                            o_src = wk[4 if c < 2 else 1][:, (c % 2) * RDV:(c % 2 + 1) * RDV]
                            ins = eng.tensor_scalar(ron[:, c, :], o_src, bmv[:, c, 0:1], brs[:, 1, c:c + 1],
                                                    ALU.subtract, ALU.mult)
                        ins.then_inc(ron_ok.sem, 1)
                        for e in range(2):
                            eng.wait_ge(rob_ps.sem, rob_ps.after(t, 2 * hf + e + 1))
                            eng.scalar_tensor_tensor(
                                out=o_all[:, bass.ds(h * 2 + e, 1), seg].rearrange("p k t -> p (k t)"),
                                in0=wk[2 + e][:, :], scalar=0.5, in1=rsz[:, e, seg],
                                op0=ALU.mult, op1=ALU.mult).then_inc(rob_ok.sem, 1)

                merge(1)

                for j in range(KT):
                    idx = BLK_OUT + j
                    if j < KT - 1:
                        split_w(n + idx + 1, (idx + 1) % 2)
                    for b in range(NHALF):
                        eng.wait_ge(dense_ok[b].sem, dense_ok[b].after(n + idx, 1))
                        eng.wait_ge(xo_in[b].sem, xo_in[b].after(l * KT + j, 16))
                        if j == 0:
                            eng.wait_ge(ol_ok.sem, ol_ok.after(l * (2 * KT) + 2 * KT - 1, 1))
                        eng.scalar_tensor_tensor(out=o_all[:, j, b * HALF:(b + 1) * HALF], in0=dense_ps[:, b, :],
                                                 scalar=0.5, in1=y1[:, b, :], op0=ALU.mult, op1=ALU.add)\
                           .then_inc(xn_ok.sem, 1)
                        eng.wait_ge(xn_ok.sem, xn_ok.after(l * KT + j, b + 1))
                        eng.sem_inc(dense_free[b].sem, 1)
            eng.wait_ge(xn_st.sem, xn_st.after(DEPTH - 1, 32))
            norm_apply(DEPTH, True)

        @block.gpsimd
        def _(eng):
            def split_w(g, slot, inc=1):
                eng.wait_ge(w_hi_ok.sem, w_hi_ok.after(g, inc))
                eng.tensor_tensor(w_lo[:, slot, :, :], w_raw[:, :, :], w_hi[:, slot, :, :].bitcast(F32), ALU.subtract)\
                   .then_inc(w_lo_ok.sem, inc)

            eng.memset(negh[:, :], -0.5).then_inc(pool_set, 1)
            eng.wait_ge(pool_set, 1)
            with eng.Fori(0, DEPTH) as lay:
                l = eng.snap(lay)
                n = eng.snap(lay * NBLK)
                split_w(n + BLK_BA, 0, 2)
                for k in range(KT):
                    eng.wait_ge(n_hi.sem, n_hi.after(l, k + 1))
                    eng.tensor_tensor(act_lo[:, k, :], hfull[:, k % 2, :], act_hi[:, k, :].bitcast(F32), ALU.subtract)\
                       .then_inc(n_lo.sem, 1)
                split_w(n + BLK_KVQ0, 0)
                for j in range(3):
                    split_w(n + BLK_KVQ0 + j + 1, (j + 1) % 2)

                def delta_head(h, last):
                    t = eng.snap(l * DH + h)
                    m = eng.snap(n + h * 6)

                    for hf in range(NHALF):
                        cs = slice(CPH * hf, CPH * hf + CPH)
                        pieces = 0

                        def per_token(ap):
                            return ap.unsqueeze(2).to_broadcast([P, CPH, P])

                        gcb3 = gcb.rearrange("p (c t) -> p c t", c=CPH)
                        for step in deltanet_schedule(hf, 16 * (3 if hf == 0 or not last else 0)):
                            what = step[0]
                            if what == "fill":
                                for i in range(pieces // KT, (pieces + step[1]) // KT):
                                    if i % 2 == 0:
                                        idx = BLK_HEADS + 3 * hf + i // 2
                                        split_w(m + idx + 1, (idx + 1) % 2)
                                pieces += step[1]
                            elif what == "tokens":
                                eng.wait_ge(row_in[0].sem, row_in[0].after(t, 16 * hf + 16))
                                eng.wait_ge(xT_ok.sem, xT_ok.after(t, 7 * hf - 6))
                                eng.tensor_tensor(t0, gcb3, bcast4(mk[:, C_NEG:C_NEG + P]), ALU.add)\
                                   .then_inc(dif_ok.sem, 1)
                                eng.wait_ge(hs_ok.sem, hs_ok.after(t, 1))
                                eng.wait_ge(dif_ok.sem, dif_ok.after(t, 2 * hf + 1))
                                eng.tensor_tensor(t0, t0, per_token(hs[:, 1, cs]), ALU.subtract)\
                                   .then_inc(dif_ok.sem, 1)
                                eng.wait_ge(nrm_s.sem, nrm_s.after(t, hf + 1))
                                eng.wait_ge(on_ok.sem, on_ok.after(t, hf))
                                eng.tensor_tensor(nrm[:, 1, :], nrm[:, 0, :], negh[:, 0:8], ALU.pow)\
                                   .then_inc(nrm_p.sem, 1)
                                eng.wait_ge(dec_ok.sem, dec_ok.after(t, hf + 1))
                                eng.wait_ge(row_in[1].sem, row_in[1].after(t, 16 * hf + 16))
                                eng.tensor_tensor(decb, dec, beb.rearrange("p (c t) -> p c t", c=CPH), ALU.mult)\
                                   .then_inc(decb_ok.sem, 1)
                                eng.wait_ge(egc_ok.sem, egc_ok.after(t, hf + 1))
                                eng.wait_ge(o_ps.sem, o_ps.after(t, CPH * hf))
                                eng.tensor_tensor(qd, kqv[:, 1, hf * HALF:(hf + 1) * HALF]
                                                  .rearrange("p (c t) -> p c t", c=CPH), egc, ALU.mult)\
                                   .then_inc(qd_ok.sem, 1)
                                eng.wait_ge(kh_ok.sem, kh_ok.after(t, hf + 1))
                                eng.tensor_tensor(kw, kh, per_token(hs[:, 2, cs]), ALU.mult).then_inc(kw_ok.sem, 1)
                                eng.tensor_tensor(kd, kh, per_token(hs[:, 3, cs]), ALU.mult).then_inc(kd_ok.sem, 1)
                            elif what == "state_out" and step[1] == CPH - 1:
                                eng.wait_ge(og_s.sem, og_s.after(t, 4 * hf + 4))
                                eng.tensor_tensor(og[:, 4, :], og[:, 3, :], negh[:, 0:CPH], ALU.pow).then_inc(og_p.sem, 1)

                with eng.Fori(0, DH - 1) as h:
                    delta_head(h, False)
                delta_head(DH - 1, True)

                def merge(a):
                    for k in range(KT):
                        g = l * (2 * KT) + (a * KT + k)
                        eng.wait_ge(oh_ok.sem, oh_ok.after(g, 1))
                        eng.tensor_tensor(o_lo[:, k, :], o_all[:, k, :], o_hi[:, k, :].bitcast(F32), ALU.subtract)\
                           .then_inc(ol_ok.sem, 1)
                    for j in range(KT):
                        idx = (BLK_UPR if a else BLK_UPD) + j
                        split_w(n + idx + 1, (idx + 1) % 2)
                        if a:
                            for b in range(NHALF):
                                seg = slice(b * HALF, (b + 1) * HALF)
                                eng.wait_ge(yh_ok.sem, yh_ok.after(l * KT + j, b + 1))
                                eng.tensor_tensor(act_lo[:, j, seg], yf[:, b, :], act_hi[:, j, seg].bitcast(F32),
                                                  ALU.subtract).then_inc(yl_ok.sem, 1)

                merge(0)
                with eng.Fori(0, RH) as h:
                    t = eng.snap(l * RH + h)
                    m = eng.snap(n + h * 6)
                    for j in range(6):
                        split_w(m + BLK_RET + j + 1, (BLK_RET + j + 1) % 2)
                    for hf in range(NHALF):
                        eng.wait_ge(rbn.sem, rbn.after(t, 10 * hf + 10))
                        eng.tensor_tensor(brs[:, 1, :], brs[:, 0, :], negh[:, 0:CPH], ALU.pow).then_inc(rpw.sem, 1)
                merge(1)
                for j in range(KT - 1):
                    split_w(n + BLK_OUT + j + 1, (BLK_OUT + j + 1) % 2)


_INS = ["x", "norm_gain", "w_in", "conv_w", "a_log", "dt_bias", "dn_norm_gain", "w_up_ret", "w_up_dn", "w_out",
        "final_gain"]


def kernel(**inputs):
    import concourse.bacc as bacc
    from concourse.bass_utils import run_bass_kernel_spmd

    nc = bacc.Bacc("TRN2", target_bir_lowering=False, num_devices=1)
    arrays, args = {}, []
    given = {name: np.ascontiguousarray(inputs[name]) for name in _INS}
    given.update(constants())
    for name, a in given.items():
        arrays[f"in_{name}"] = a
        args.append(nc.dram_tensor(f"in_{name}", a.shape, mybir.dt.from_np(a.dtype), kind="ExternalInput").ap())
    out = nc.dram_tensor("out_0", [1, SEQ, D_MODEL], F32, kind="ExternalOutput").ap()
    build(nc, *args, out)
    r = run_bass_kernel_spmd(nc, [arrays], core_ids=[0])
    return r.results[0]["out_0"]
```

```python
from contextlib import ExitStack

import numpy as np
import concourse.bass as bass
from concourse import mybir

F32 = mybir.dt.float32
F32R = mybir.dt.float32r
ALU = mybir.AluOpType
ACT = mybir.ActivationFunctionType

P = 128
D_MODEL, SEQ, DEPTH = 1024, 1024, 2
KT = D_MODEL // P
HALF = 512
NHALF = SEQ // HALF
CPH = HALF // P
NCH = SEQ // P
RH, RDV = 4, 256
DH = 8
DK = 128
TAPS = 4
EPS = 1e-6
IN_W = 9232
RQ0, RK0, RV0, RZ0 = 0, 512, 1024, 2048
DQ0, DK0, DV0, DZ0 = 3072, 4096, 5120, 6144
BA0, GR0, GD0 = 7168, 7184, 8208
LEVELS = [2, 4, 8, 16, 32, 64]
HBUF = 4

BLK_BA, BLK_KVQ0, BLK_HEADS = 0, 2, 5
BLK_UPD = BLK_HEADS + 6 * DH - 3
BLK_RET = BLK_UPD + KT
BLK_UPR = BLK_RET + 6 * RH
BLK_OUT = BLK_UPR + KT
NBLK = BLK_OUT + KT

C_ID, C_UP, C_NEG, C_M1, C_LV, C_ONE = 0, P, 2 * P, 3 * P, 4 * P, 10 * P
C_ALL = 11 * P
ROW_CONV, ROW_NG, ROW_DN, ROW_FG = 0, 96, 104, 105
ROWS = 113
ARENA = 21056


class Signal:

    def __init__(self, handle, per):
        self.sem, self.per = handle, per

    def after(self, t, k):
        return t * self.per + (self.per + k)


def constants():
    i = np.arange(P)
    row, col = i[:, None], i[None, :]
    parts = [row == col, row <= col, np.where(col >= row, 0.0, -1e30), -1.0 * ((col == row + 1) & (row % 2 == 0))]
    for s in LEVELS:
        parts.append((row // (2 * s) == col // (2 * s)) & (row % (2 * s) >= s) & (col % (2 * s) < s))
    parts.append(np.ones((P, P)))
    masks = np.concatenate([np.asarray(p, np.float32) for p in parts], 1)
    half = DK // 2
    inv = np.power(np.float32(10000.0), -np.arange(half, dtype=np.float32) / np.float32(half)).astype(np.float32)
    ang = (np.arange(SEQ, dtype=np.float32)[:, None] * inv[None, :]).astype(np.float32).T
    cos, sin = np.cos(ang), np.sin(ang)
    rope = np.stack([np.concatenate([cos, cos]), np.concatenate([-sin, sin])], 1).astype(np.float32)
    ret = np.zeros((RH, P, 2 * P + 2), np.float64)
    for h in range(RH):
        lg = np.log1p(-(2.0 ** (-5 - h)))
        ret[h, :, 0:P] = np.where(col >= row, np.exp(np.maximum(col - row, 0) * lg), 0) * DK ** -0.5
        ret[h, :, P:2 * P] = np.exp((col + 1.0) * lg)
        ret[h, :, 2 * P] = np.exp((P - 1 - i) * lg) * DK ** -0.5
        ret[h, :, 2 * P + 1] = np.exp(P * lg)
    return {"masks": masks, "rope": rope.reshape(P, 2 * SEQ), "ret": ret.astype(np.float32)}


def deltanet_schedule(hf, fills):
    s = [("tokens",), 7, ("khat_back",), 2, ("grams",), 3, ("x_first",), 1]
    for n in range(len(LEVELS)):
        s += [("inv_y", n), 1, ("inv_xt", n), 1]
        if n < len(LEVELS) - 1:
            s += [("inv_x", n), 1]
    s += [("w",), 2]
    for c in range(CPH):
        s += [("v_new", c), 1, ("state_out", c), 1]
    s += [7, ("o_back",)]
    steps, left = [], fills
    for x in s:
        if isinstance(x, int):
            x = min(x, left)
            left -= x
            if x:
                steps.append(("fill", x))
        else:
            steps.append(x)
    if left:
        steps.insert(len(steps) - 1, ("fill", left))

    def taps(i):
        return [("conv", i, k) for k in range(TAPS)] + [("tanh", i)]

    out, pieces, waiting = [], 0, taps(5) if hf == 0 else []

    def spread(n):
        nonlocal waiting
        silus = []
        while waiting and n > 0:
            x = waiting.pop(0)
            out.append(x)
            if x[0] == "tanh":
                silus.append(("silu", x[1]))
            else:
                n -= 1
        waiting = silus + waiting

    for n, x in enumerate(steps):
        out.append(x)
        if x[0] == "fill":
            if ("o_back",) in steps[n + 1:n + 3]:
                spread(6)
            for i in range(pieces // KT, (pieces + x[1]) // KT):
                out.append(("evac", i))
                if i % 2 == 0:
                    waiting.insert(0, ("split", i // 2))
                if hf == 0 and i < 2:
                    waiting.append(("z_silu", i))
                if hf == 1 and i < 5:
                    if i == 4:
                        waiting = taps(i) + waiting
                    else:
                        waiting += taps(i)
            pieces += x[1]
        else:
            spread({"tokens": 2, "khat_back": 3, "x_first": 2, "inv_x": 2}.get(x[0], 1))
    while waiting:
        spread(1)
    return out


def build(nc, x, norm_gain, w_in, conv_w, a_log, dt_bias, dn_gain, w_up_ret, w_up_dn, w_out, final_gain,
          masks, rope, ret, out):
    ctx = ExitStack()
    with ctx:
        def sb(name, shape, dt=F32):
            return ctx.enter_context(nc.sbuf_tensor(name, shape, dt))

        def signal(name, per):
            s = Signal(ctx.enter_context(nc.semaphore(name)), per)
            signals.append(s)
            return s

        def plain(name):
            return ctx.enter_context(nc.semaphore(name))

        signals = []

        act_hi = sb("act_hi", [P, KT, SEQ], F32R)
        act_lo = sb("act_lo", [P, KT, SEQ], F32R)
        o_all = sb("o_all", [P, KT, SEQ])
        w_raw = sb("w_raw", [P, KT, P])
        w_hi = sb("w_hi", [P, 2, KT, P], F32R)
        w_lo = sb("w_lo", [P, 2, KT, P], F32R)
        mk = sb("mk", [P, C_ALL])
        cols = sb("cols", [P, P])
        small = sb("small", [P, 4, DH, NCH])
        g_tok = sb("g_tok", [P, NCH, DH])
        abias = sb("abias", [P, 3, DH])
        dngh = sb("dngh", [P, 1])
        negh = sb("negh", [P, 16])
        arena_at = -(-nc.sbuf_base // 32) * 32
        arena = sb("arena", [P, ARENA])
        ident, upper, ones = mk[:, C_ID:C_ID + P], mk[:, C_UP:C_UP + P], mk[:, C_ONE:C_ONE + P]

        ident2 = ident.unsqueeze(1).to_broadcast([P, 2, P])

        X_BANKS, Y_BANKS, XT_BANKS = (2, 3), (0, 4), (1, 5)

        def paired(banks, c):
            return wk[banks[c // 2]][:, (c % 2) * P:(c % 2 + 1) * P]

        def pair_of(banks, c):
            return wk[banks[c // 2]][:, 0:2 * P].rearrange("p (c t) -> p c t", c=2)

        def pair(n, c):
            return 2 * n + c // 2 + 1

        def bcast4(ap):
            return ap.unsqueeze(1).to_broadcast([P, CPH, P])

        place = {"at": 0}

        def plan():
            place["at"] = 0

        def ar(name, shape, dt=F32):
            n = int(np.prod(shape[1:]))
            a = place["at"]
            place["at"] = a + n
            assert place["at"] <= ARENA, (name, place)
            if dt is F32:
                v = arena[:, a:a + n]
                if len(shape) == 3:
                    v = v.rearrange("p (a b) -> p a b", a=shape[1])
                if len(shape) == 4:
                    v = v.rearrange("p (a b c) -> p a b c", a=shape[1], b=shape[2])
                return v
            return nc.alloc_sbuf_tensor_at(name, shape, dt, offset=arena_at + 4 * a)

        plan()
        raw = ar("raw", [P, 2, SEQ + 4])
        acc = ar("acc", [P, 2, HALF])
        th = ar("th", [P, 2, HALF])
        kqv = ar("kqv", [P, 3, SEQ])
        sz = ar("sz", [P, SEQ])
        gate_t = ar("gate_t", [P, 2, HALF])
        sq = ar("sq", [P, 2, HALF])
        gcb = ar("gcb", [P, HALF])
        beb = ar("beb", [P, HALF])
        hs = ar("hs", [P, 4, NCH])
        nrm = ar("nrm", [P, 4, 8])
        ssum = ar("ssum", [P, 2 * CPH])
        kh, khT, kd, kw, vb = (ar(n, [P, CPH, P]) for n in ("kh", "khT", "kd", "kw", "vb"))
        dec, decb, egc, qd = (ar(n, [P, CPH, P]) for n in ("dec", "decb", "egc", "qd"))
        lT, aT, xT, xx, yy, nw = (ar(n, [P, CPH, P]) for n in ("lT", "aT", "xT", "xx", "yy", "nw"))
        t0 = ar("t0", [P, CPH, P])
        on = ar("on", [P, CPH, P])
        vn = ar("vn", [P, 2, P])
        state = ar("state", [P, 2, P])
        og = ar("og", [P, 6, CPH])
        plan()
        rope_t = ar("rope_t", [P, 2, SEQ])
        swap = ar("swap", [P, 2, HALF])
        rt1 = ar("rt1", [P, HALF])
        rt2 = ar("rt2", [P, HALF])
        rkq = ar("rkq", [P, 2, SEQ])
        rvT = ar("rvT", [P, 2, SEQ])
        rth = ar("rth", [P, 2, HALF])
        rsz = ar("rsz", [P, 2, SEQ])
        rcon = ar("rcon", [P, 2 * P + 2])
        rkd, rqd, rsc = (ar(n, [P, CPH, P]) for n in ("rkd", "rqd", "rsc"))
        rvt = ar("rvt", [P, CPH, RDV])
        ron = ar("ron", [P, CPH, RDV])
        rstate = ar("rstate", [P, 2, RDV])
        bst = ar("bst", [P, CPH, 6])
        bmv = ar("bmv", [P, CPH, 2])
        brs = ar("brs", [P, 2, CPH])
        plan()
        o_hi = ar("o_hi", [P, KT, SEQ], F32R)
        o_lo = ar("o_lo", [P, KT, SEQ], F32R)
        gy = ar("gy", [P, 2, HALF])
        y1 = ar("y1", [P, 2, HALF])
        yf = ar("yf", [P, 2, HALF])
        plan()
        nsq = ar("nsq", [P, 2, SEQ])
        ssq = ar("ssq", [P, SEQ])
        ms = ar("ms", [P, SEQ])
        r0 = ar("r0", [P, SEQ])
        r1 = ar("r1", [P, SEQ])
        xin = ar("xin", [P, 2, D_MODEL])
        prow = arena[0:ROWS, place["at"]:place["at"] + P]
        place["at"] += P
        final_x = ar("final_x", [P, KT, SEQ])
        place["at"] -= KT * SEQ
        hfull = ar("hfull", [P, HBUF, SEQ])
        ba = arena[0:16, place["at"]:place["at"] + SEQ]
        place["at"] += SEQ
        btk = ar("btk", [P, NCH, 16])
        sp = ar("sp", [P, 4, NCH * DH])
        rows8 = arena[0:DH, place["at"]:place["at"] + 2 * SEQ].rearrange("p (a b) -> p a b", a=2)
        place["at"] += 2 * SEQ

        dense_ps = ctx.enter_context(nc.psum_tensor("dense_ps", [P, 2, HALF], F32))
        wk = [ctx.enter_context(nc.psum_tensor(f"work{n}", [P, HALF], F32)) for n in range(6)]

        def chunks(bank):
            return wk[bank][:, :].rearrange("p (c t) -> p c t", c=CPH)

        x_dram = nc.dram_tensor("x_scratch", [KT, P, SEQ], F32)
        gate_dram = nc.dram_tensor("gate_scratch", [2, KT, P, SEQ], F32)
        y_dram = nc.dram_tensor("y_scratch", [KT, P, SEQ], F32)
        row_dram = nc.dram_tensor("row_scratch", [2, DH, SEQ], F32)

        const_in = plain("const_in")
        waited = plain("waited")
        prow_in = plain("prow_in")
        cols_ps, cols_ok = plain("cols_ps"), plain("cols_ok")
        xin_in = [plain("xin_in0"), plain("xin_in1")]
        xin_ps, xin_ok = plain("xin_ps"), plain("xin_ok")
        x0_stored = plain("x0_stored")
        out_ps, out_ok, out_stored = plain("out_ps"), plain("out_ok"), [plain("out_stored0"), plain("out_stored1")]
        pool_set = plain("pool_set")
        halo_ok = signal("halo_zeroed", 1)
        w_in_ok = signal("w_loaded", 16)
        w_hi_ok, w_lo_ok = signal("w_hi_ready", 1), signal("w_lo_ready", 1)
        dense_ok = [signal("dense_done0", 1), signal("dense_done1", 1)]
        dense_free = [signal("dense_free0", 1), signal("dense_free1", 1)]
        n_sq = signal("norm_squares", KT)
        n_add = signal("norm_squares_added", KT)
        n_ps = signal("norm_sums", 2)
        n_step = signal("norm_steps", 10)
        n_act = signal("norm_act", 4)
        n_full = signal("norm_scaled", KT)
        n_hi = signal("norm_hi", KT)
        n_lo = [signal("norm_lo_even", KT // 2), signal("norm_lo_odd", KT // 2)]
        b_in = signal("abias_loaded", 32)
        b_row = signal("ba_rows", 2)
        b_tokps = signal("ba_tokens_psum", 1)
        b_dve, b_act = signal("ba_vector", 8), signal("ba_scalar", 8)
        b_gcps, b_rowps, b_rows = signal("gc_psum", 1), signal("rows_psum", 2), signal("rows_ready", 2)
        b_st = signal("rows_stored", 16)
        raw_ok = signal("raw_ready", 6)
        conv_s = signal("conv_steps", 24)
        th_ok = signal("tanh_ready", 8)
        kqv_ok = signal("kqv_ready", 6)
        sz_ok = signal("z_silu_ready", 2)
        gt_ok = signal("gate_tanh_ready", 4)
        gt_st = [signal("gate_stored0", 32), signal("gate_stored1", 32)]
        row_in = [signal("gc_row_loaded", 32), signal("beta_row_loaded", 32)]
        hs_ok = signal("head_scalars", 1)
        sq_ok = signal("squares_ready", 4)
        tok_ps, kq_ps = signal("tokens_psum", 2), signal("kq_tokens_psum", 4)
        sqr_ok = signal("squares_summed", 4)
        nrm_s, nrm_p = signal("norms_ready", 4), signal("norm_power", 4)
        kh_ok, vb_ok = signal("khat_ready", 2), signal("vbeta_ready", 2)
        khb_ps, khT_ok = signal("khat_back_psum", 2), signal("khatT_ready", 2)
        kw_ok, kd_ok = signal("k_w_ready", 2), signal("k_dec_ready", 2)
        dif_ok, dec_ok, decb_ok = signal("gc_diff", 4), signal("decay_ready", 2), signal("decay_beta_ready", 2)
        egc_ok, qd_ok = signal("exp_gc_ready", 2), signal("q_dec_ready", 2)
        gram_ps = signal("grams_psum", 2)
        lT_ok, aT_ok, l1_ok = signal("lT_ready", 2), signal("attnT_ready", 2), signal("l1_ready", 4)
        dm_ok = signal("decay_pairs_ready", 2)
        xT_ok, x_ps, x_ok = signal("xT_ready", 28), signal("x_psum", 24), signal("x_ready", 24)
        y_ps, y_ok, xt_ps = signal("y_psum", 24), signal("y_ready", 24), signal("xt_psum", 24)
        w_ps, nw_ok = signal("w_psum", 2), signal("neg_w_ready", 2)
        vn_ps, vn_ok = signal("v_new_psum", 8), signal("v_new_ready", 8)
        st_ps, st_ok = signal("state_psum", 8), signal("state_ready", 8)
        o_ps = signal("o_psum", 8)
        osq_ok, og_s, og_p, on_ok = signal("o_squares", 2), signal("o_norm_steps", 8), signal("o_power", 2), signal("o_normed", 2)
        ob_ps, ob_ok = signal("o_back_psum", 2), signal("o_ready", 2)
        rgl = signal("o_scale", 2)
        rope_in = signal("rope_loaded", 16)
        rc_in = signal("ret_consts_loaded", 16)
        swap_ok = signal("swap_ready", 8)
        rrot, rpart = signal("rope_parts", 8), signal("rope_ready", 4)
        rv_ok, rth_ok, rsz_ok = signal("rv_ready", 4), signal("rz_tanh", 4), signal("rz_silu", 4)
        rtok_ps = signal("ret_tokens_psum", 4)
        rkd_ok, rvt_ok, rqd_ok = signal("ret_kdec", 2), signal("ret_vtok", 4), signal("ret_qdec", 2)
        rsc_ps, rsc_ok = signal("ret_scores_psum", 2), signal("ret_scores", 2)
        rkv_ps, rst_ok = signal("ret_kv_psum", 8), signal("ret_state", 8)
        ro_ps, rbn = signal("ret_o_psum", 8), signal("ret_stats", 20)
        rpw, ron_ok = signal("ret_rstd", 2), signal("ret_o_normed", 2)
        rob_ps, rob_ok = signal("ret_o_back_psum", 4), signal("ret_o_ready", 4)
        oh_ok = signal("o_hi_ready", KT)
        ol_ok = [signal("o_lo_even", KT // 2), signal("o_lo_odd", KT // 2)]
        g_in = [signal("gate_loaded0", 16), signal("gate_loaded1", 16)]
        y_in = [signal("y_loaded0", 16), signal("y_loaded1", 16)]
        y_st = [signal("y_stored0", 16), signal("y_stored1", 16)]
        yg_ok, yf_ok = signal("y_gated", 2), signal("y_merged", 2)
        yh_ok, yl_ok = signal("y_hi", 2), signal("y_lo", 2)
        xo_in = [signal("x_loaded0", 16), signal("x_loaded1", 16)]
        xn_ok = signal("x_new", 2)
        xn_st = signal("x_stored", 32)

        def settled(eng):
            eng.sem_inc(waited, 1)

        block = ctx.enter_context(nc.Block())

        def w_src(t, what, col=0):
            return what[t, :, bass.ds(col, P)].rearrange("(k p) n -> p k n", p=P)

        @block.sync
        def _(eng):
            for s in signals:
                eng.sem_inc(s.sem, s.per)
            eng.dma_start(mk[:, :], masks).then_inc(const_in, 16)
            cw = conv_w

            def load_w(g, src, parts=1):
                eng.wait_ge(w_lo_ok.sem, w_lo_ok.after(g, 0))
                settled(eng)
                for a in range(parts):
                    ks = slice(a * KT // parts, (a + 1) * KT // parts)
                    eng.dma_start(w_raw[:, ks, :], src[:, ks, :]).then_inc(w_in_ok.sem, 16)

            for i in range(NCH):
                if i >= 2:
                    eng.wait_ge(xin_ps, i - 1)
                eng.dma_start(xin[:, i % 2, :], x[0, i * P:(i + 1) * P, :]).then_inc(xin_in[i % 2], 16)
            eng.wait_ge(xin_ok, 2 * NCH)
            eng.dma_start(x_dram[:, :, :].rearrange("k p t -> p k t"), o_all[:, :, :]).then_inc(x0_stored, 16)

            with eng.Fori(0, DEPTH) as lay:
                l = eng.snap(lay)
                n = eng.snap(lay * NBLK)
                eng.wait_ge(n_hi.sem, n_hi.after(l, 0))
                settled(eng)
                eng.wait_ge(xn_ok.sem, xn_ok.after(l * KT, 0))
                settled(eng)
                eng.dma_start(prow[ROW_CONV:ROW_CONV + 96, :],
                              cw[l].rearrange("k (b c) -> (k b) c", c=P)).then_inc(prow_in, 16)
                eng.dma_start(prow[ROW_NG:ROW_NG + KT, :],
                              norm_gain[l].rearrange("(k p) -> k p", p=P)).then_inc(prow_in, 16)
                eng.dma_start(prow[ROW_DN:ROW_DN + 1, :],
                              dn_gain[l].rearrange("(k p) -> k p", p=P)).then_inc(prow_in, 16)
                eng.dma_start(prow[ROW_FG:ROW_FG + KT, :],
                              final_gain.rearrange("(k p) -> k p", p=P)).then_inc(prow_in, 16)
                eng.dma_start(abias[:, 0, :], dt_bias[l].unsqueeze(0).to_broadcast([P, DH])).then_inc(b_in.sem, 16)
                eng.dma_start(abias[:, 1, :], a_log[l].unsqueeze(0).to_broadcast([P, DH])).then_inc(b_in.sem, 16)
                load_w(n + BLK_BA, w_src(l, w_in, BA0), 2)
                for j, c0 in enumerate((DK0, DV0, DQ0)):
                    load_w(n + BLK_KVQ0 + j, w_src(l, w_in, c0))
                eng.wait_ge(b_rows.sem, b_rows.after(l, 2))
                settled(eng)
                eng.dma_start(row_dram[:, :, :].rearrange("a h t -> h a t"), rows8).then_inc(b_st.sem, 16)
                eng.wait_ge(b_st.sem, b_st.after(l, 16))
                settled(eng)

                def head_loads(h, last):
                    t = eng.snap(l * DH + h)
                    m = eng.snap(n + h * 6)
                    rows = [row_dram[a, bass.ds(h, 1), :] for a in range(2)]
                    for hf in range(NHALF):
                        eng.wait_ge(egc_ok.sem, egc_ok.after(t, hf))
                        settled(eng)
                        eng.wait_ge(dif_ok.sem, dif_ok.after(t, 2 * hf))
                        settled(eng)
                        for a, dst in enumerate((gcb, beb)):
                            if a:
                                eng.wait_ge(decb_ok.sem, decb_ok.after(t, hf))
                                settled(eng)
                            eng.dma_start(dst, rows[a][:, hf * HALF:(hf + 1) * HALF].to_broadcast([P, HALF]))\
                               .then_inc(row_in[a].sem, 16)
                        if hf == 0:
                            for j, c0 in enumerate((DZ0, GD0, GR0)):
                                load_w(m + BLK_HEADS + j, w_src(l, w_in, c0 + h * P))
                        elif not last:
                            for j, c0 in enumerate((DK0, DV0, DQ0)):
                                load_w(m + BLK_HEADS + 3 + j, w_src(l, w_in, c0 + P + h * P))

                with eng.Fori(0, DH - 1) as h:
                    head_loads(h, False)
                head_loads(DH - 1, True)

                for j in range(KT):
                    load_w(n + (BLK_UPD + j), w_src(l, w_up_dn, j * P))
                with eng.Fori(0, RH) as h:
                    t = eng.snap(l * RH + h)
                    m = eng.snap(n + h * 6 + BLK_RET)
                    load_w(m, w_src(l, w_in, RK0 + h * P))
                    load_w(m + 1, w_src(l, w_in, RQ0 + h * P))
                    for j in range(2):
                        load_w(m + 2 + j, w_src(l, w_in, RV0 + j * P + h * RDV))
                    for j in range(2):
                        load_w(m + 4 + j, w_src(l, w_in, RZ0 + j * P + h * RDV))
                    eng.wait_ge(rst_ok.sem, rst_ok.after(t, 0))
                    settled(eng)
                    eng.wait_ge(rsc_ok.sem, rsc_ok.after(t, 0))
                    settled(eng)
                    eng.wait_ge(rqd_ok.sem, rqd_ok.after(t, 0))
                    settled(eng)
                    eng.dma_start(rcon, ret[bass.ds(h, 1), :, :].rearrange("h p n -> p (h n)")).then_inc(rc_in.sem, 16)

                for j in range(KT):
                    load_w(n + (BLK_UPR + j), w_src(l, w_up_ret, j * P))
                for j in range(KT):
                    load_w(n + (BLK_OUT + j), w_src(l, w_out, j * P))
                eng.wait_ge(xn_ok.sem, xn_ok.after(l * KT + KT - 1, 2))
                settled(eng)
                for c in range(2):
                    eng.dma_start(x_dram[4 * c:4 * c + 4, :, :].rearrange("k p t -> p k t"),
                                  o_all[:, 4 * c:4 * c + 4, :]).then_inc(xn_st.sem, 16)
            for i in range(NCH):
                eng.wait_ge(out_ok, 2 * i + 2)
                eng.dma_start(out[0, i * P:(i + 1) * P, :], xin[:, i % 2, :]).then_inc(out_stored[i % 2], 16)
            for s in out_stored:
                eng.wait_ge(s, 16 * NCH // 2)
            eng.wait_ge(xn_st.sem, xn_st.after(DEPTH - 1, 32))
            settled(eng)

        @block.tensor
        def _(eng):
            def turn(bank, blocks):
                for c, src in enumerate(blocks):
                    mm = eng.transpose(wk[bank][:, c * P:(c + 1) * P], src, ident)
                return mm

            def dense_pieces(g, slot, hi, lo, inc=1, ready=None, halves=range(NHALF)):
                for b in halves:
                    seg = slice(b * HALF, (b + 1) * HALF)
                    for k in range(KT):
                        if k == 0:
                            if b == halves[0]:
                                eng.wait_ge(w_lo_ok.sem, w_lo_ok.after(g, 1))
                            eng.wait_ge(dense_free[b].sem, dense_free[b].after(g, 0))
                        if ready is not None and b == 0:
                            eng.wait_ge(*ready(k))
                        eng.matmul(dense_ps[:, b, :], w_hi[:, slot, k, :], hi[:, k, seg],
                                   start=(k == 0), stop=False)
                        eng.matmul(dense_ps[:, b, :], w_hi[:, slot, k, :], lo[:, k, seg],
                                   start=False, stop=False)
                        mm = eng.matmul(dense_ps[:, b, :], w_lo[:, slot, k, :], hi[:, k, seg],
                                        start=False, stop=(k == KT - 1))
                        if k == KT - 1:
                            mm.then_inc(dense_ok[b].sem, inc)
                        yield

            def dense(*a, **kw):
                for _ in dense_pieces(*a, **kw):
                    pass

            eng.wait_ge(const_in, 16)
            for i in range(NCH):
                eng.wait_ge(xin_in[i % 2], 16 * (i // 2 + 1))
                for a in range(2):
                    if i >= 1:
                        eng.wait_ge(xin_ok, 2 * i - 1 + a)
                    mm = turn(a, [xin[:, i % 2, (4 * a + c) * P:(4 * a + c + 1) * P] for c in range(4)])
                    if a == 1:
                        mm.then_inc(xin_ps, 1)
                    else:
                        mm.then_inc(out_ps, 1)

            def norm_sums(t):
                eng.wait_ge(n_add.sem, n_add.after(t, KT))
                for b in range(NHALF):
                    eng.matmul(wk[b][:, :], ones, ssq[:, b * HALF:(b + 1) * HALF], start=True, stop=True)\
                       .then_inc(n_ps.sem, 1)

            with eng.Fori(0, DEPTH) as lay:
                l = eng.snap(lay)
                n = eng.snap(lay * NBLK)
                eng.wait_ge(prow_in, l * 64 + 64)
                settled(eng)
                eng.transpose(wk[2][:, 0:ROWS], prow, ident[0:ROWS, 0:ROWS]).then_inc(cols_ps, 1)
                norm_sums(l)
                dense(n + BLK_BA, 0, act_hi, act_lo, 2, lambda k: (n_lo[k % 2].sem, n_lo[k % 2].after(l, k // 2 + 1)))

                eng.wait_ge(b_row.sem, b_row.after(l, 2))
                settled(eng)
                for c in range(NCH):
                    mm = eng.transpose(wk[3][:, 16 * c:16 * c + 16], ba[:, c * P:(c + 1) * P], ident[0:16, 0:16])
                mm.then_inc(b_tokps.sem, 1)
                dense(n + BLK_KVQ0, 0, act_hi, act_lo)
                eng.wait_ge(b_dve.sem, b_dve.after(l, 6))
                eng.matmul(wk[4][:, 0:64], upper, g_tok[:, :, :].rearrange("p c h -> p (c h)"), start=True, stop=True)
                eng.matmul(wk[4][:, 64:128], ones, g_tok[:, :, :].rearrange("p c h -> p (c h)"), start=True, stop=True)\
                   .then_inc(b_gcps.sem, 1)
                eng.wait_ge(b_act.sem, b_act.after(l, 7))
                for a in range(2):
                    for c in range(NCH):
                        if a and c == 0:
                            eng.wait_ge(b_rows.sem, b_rows.after(l, 1))
                        mm = eng.transpose(wk[c // 4][0:DH, (c % 4) * P:(c % 4 + 1) * P],
                                           small[:, 1 - a, :, c], ident)
                    mm.then_inc(b_rowps.sem, 1)
                for j in range(1, 3):
                    dense(n + BLK_KVQ0 + j, j % 2, act_hi, act_lo)

                def delta_head(h, last):
                    t = eng.snap(l * DH + h)
                    m = eng.snap(n + h * 6)

                    def stream(hf):
                        js = range(3) if hf == 0 else range(0 if last else 3)
                        for j in js:
                            jj = 3 * hf + j
                            yield from dense_pieces(m + BLK_HEADS + jj, (BLK_HEADS + jj) % 2, act_hi, act_lo)

                    for hf in range(NHALF):
                        fills = stream(hf)
                        seg = slice(hf * HALF, (hf + 1) * HALF)

                        def ch(ap, c):
                            return ap[:, hf * HALF + c * P:hf * HALF + (c + 1) * P]

                        for step in deltanet_schedule(hf, 16 * (3 if hf == 0 or not last else 0)):
                            what = step[0]
                            if what == "fill":
                                for _ in range(step[1]):
                                    next(fills)
                            elif what == "tokens":
                                eng.wait_ge(kqv_ok.sem, kqv_ok.after(t, 5 + hf))
                                turn(0, [ch(kqv[:, 0, :], c) for c in range(CPH)]).then_inc(kq_ps.sem, 1)
                                turn(3, [ch(kqv[:, 1, :], c) for c in range(CPH)]).then_inc(kq_ps.sem, 1)
                                turn(4, [ch(kqv[:, 2, :], c) for c in range(CPH)]).then_inc(tok_ps.sem, 1)
                            elif what == "khat_back":
                                eng.wait_ge(kh_ok.sem, kh_ok.after(t, hf + 1))
                                turn(2, [kh[:, c, :] for c in range(CPH)]).then_inc(khb_ps.sem, 1)
                            elif what == "grams":
                                eng.wait_ge(khT_ok.sem, khT_ok.after(t, hf + 1))
                                for c in range(CPH):
                                    eng.matmul(wk[5][:, c * P:(c + 1) * P], khT[:, c, :], khT[:, c, :],
                                               start=True, stop=True)
                                for c in range(CPH):
                                    mm = eng.matmul(wk[4][:, c * P:(c + 1) * P], khT[:, c, :],
                                                    ch(kqv[:, 1, :], c), start=True, stop=True)
                                mm.then_inc(gram_ps.sem, 1)
                            elif what in ("x_first", "inv_x"):
                                i = 0 if what == "x_first" else step[1] + 1
                                for c in range(CPH):
                                    if c % 2 == 0:
                                        eng.wait_ge(xT_ok.sem, xT_ok.after(t, pair(7 * hf + i, c)))
                                    mm = eng.transpose(paired(X_BANKS, c), xT[:, c, :], ident)
                                    if c % 2:
                                        mm.then_inc(x_ps.sem, 1)
                            elif what == "inv_y":
                                i = step[1]
                                if i == 0:
                                    eng.wait_ge(lT_ok.sem, lT_ok.after(t, hf + 1))
                                    eng.wait_ge(aT_ok.sem, aT_ok.after(t, hf + 1))
                                for c in range(CPH):
                                    if c % 2 == 0:
                                        eng.wait_ge(x_ok.sem, x_ok.after(t, pair(6 * hf + i, c)))
                                    mm = eng.matmul(paired(Y_BANKS, c), lT[:, c, :], xx[:, c, :],
                                                    start=True, stop=True)
                                    if c % 2:
                                        mm.then_inc(y_ps.sem, 1)
                            elif what == "inv_xt":
                                i = step[1]
                                if i == 0:
                                    eng.wait_ge(ob_ok.sem, ob_ok.after(t, hf))
                                for c in range(CPH):
                                    if c % 2 == 0:
                                        eng.wait_ge(y_ok.sem, y_ok.after(t, pair(6 * hf + i, c)))
                                    mm = eng.matmul(paired(XT_BANKS, c), yy[:, c, :], xT[:, c, :],
                                                    start=True, stop=True)
                                    if c % 2:
                                        mm.then_inc(xt_ps.sem, 1)
                            elif what == "w":
                                eng.wait_ge(xT_ok.sem, xT_ok.after(t, 2 * (7 * hf + 7)))
                                eng.wait_ge(kw_ok.sem, kw_ok.after(t, hf + 1))
                                for c in range(CPH):
                                    mm = eng.matmul(wk[3][:, c * P:(c + 1) * P], kw[:, c, :], xT[:, c, :],
                                                    start=True, stop=True)
                                mm.then_inc(w_ps.sem, 1)
                            elif what == "v_new":
                                c = step[1]
                                cc = CPH * hf + c
                                bank = wk[4][:, (c % 2) * P:(c % 2 + 1) * P]
                                if c == 0:
                                    eng.wait_ge(nw_ok.sem, nw_ok.after(t, hf + 1))
                                    eng.wait_ge(aT_ok.sem, aT_ok.after(t, hf + 1))
                                eng.matmul(bank, xT[:, c, :], vb[:, c, :], start=True, stop=(cc == 0))
                                if cc:
                                    eng.wait_ge(st_ok.sem, st_ok.after(t, cc))
                                    mm = eng.matmul(bank, nw[:, c, :], state[:, cc % 2, :], start=False, stop=True)
                                else:
                                    mm = eng.matmul(bank, xT[:, c, :], vb[:, c, :], start=True, stop=True)
                                mm.then_inc(vn_ps.sem, 1)
                            elif what == "state_out":
                                c = step[1]
                                cc = CPH * hf + c
                                eng.wait_ge(vn_ok.sem, vn_ok.after(t, cc + 1))
                                if c == 0:
                                    eng.wait_ge(kd_ok.sem, kd_ok.after(t, hf + 1))
                                    eng.wait_ge(qd_ok.sem, qd_ok.after(t, hf + 1))
                                eng.matmul(wk[5][:, (c % 2) * P:(c % 2 + 1) * P], kd[:, c, :], vn[:, c % 2, :],
                                           start=True, stop=True).then_inc(st_ps.sem, 1)
                                dst = wk[1][:, c * P:(c + 1) * P]
                                if cc:
                                    eng.matmul(dst, qd[:, c, :], state[:, cc % 2, :], start=True, stop=False)
                                eng.matmul(dst, aT[:, c, :], vn[:, c % 2, :], start=(cc == 0), stop=True)\
                                   .then_inc(o_ps.sem, 1)
                            elif what == "o_back":
                                eng.wait_ge(on_ok.sem, on_ok.after(t, hf + 1))
                                turn(1, [on[:, c, :] for c in range(CPH)]).then_inc(ob_ps.sem, 1)
                        for _ in fills:
                            pass

                with eng.Fori(0, DH - 1) as h:
                    delta_head(h, False)
                delta_head(DH - 1, True)

                for j in range(KT):
                    dense(n + BLK_UPD + j, (BLK_UPD + j) % 2, o_hi, o_lo,
                          ready=(lambda k: (ol_ok[k % 2].sem, ol_ok[k % 2].after(l * 2, k // 2 + 1))) if j == 0 else None)

                with eng.Fori(0, RH) as h:
                    t = eng.snap(l * RH + h)
                    m = eng.snap(n + h * 6)
                    for j in range(4):
                        dense(m + BLK_RET + j, (BLK_RET + j) % 2, act_hi, act_lo)

                    def z_stream(hf):
                        for j in (4, 5):
                            yield from dense_pieces(m + BLK_RET + j, (BLK_RET + j) % 2, act_hi, act_lo,
                                                    halves=(hf,))

                    for hf in range(NHALF):
                        fills = z_stream(hf)

                        def fill(n):
                            for _ in range(n):
                                next(fills)
                        def ch(ap, c):
                            return ap[:, hf * HALF + c * P:hf * HALF + (c + 1) * P]
                        eng.wait_ge(rpart.sem, rpart.after(t, 4))
                        eng.wait_ge(rv_ok.sem, rv_ok.after(t, 4))
                        eng.wait_ge(rob_ok.sem, rob_ok.after(t, 2 * hf))
                        eng.wait_ge(ron_ok.sem, ron_ok.after(t, hf))
                        turn(0, [ch(rkq[:, 0, :], c) for c in range(CPH)]).then_inc(rtok_ps.sem, 1)
                        for c in range(CPH):
                            mm = eng.matmul(wk[1][:, c * P:(c + 1) * P], ch(rkq[:, 0, :], c), ch(rkq[:, 1, :], c),
                                            start=True, stop=True)
                        mm.then_inc(rsc_ps.sem, 1)
                        for e in range(2):
                            mm = turn(2 + e, [ch(rvT[:, e, :], c) for c in range(CPH)])
                        mm.then_inc(rtok_ps.sem, 1)
                        fill(5)
                        eng.wait_ge(rkd_ok.sem, rkd_ok.after(t, hf + 1))
                        eng.wait_ge(rvt_ok.sem, rvt_ok.after(t, 2 * hf + 2))
                        eng.wait_ge(rsc_ok.sem, rsc_ok.after(t, hf + 1))
                        eng.wait_ge(rqd_ok.sem, rqd_ok.after(t, hf + 1))
                        for c in range(CPH):
                            cc = CPH * hf + c
                            if c >= 2:
                                eng.wait_ge(rst_ok.sem, rst_ok.after(t, cc - 1))
                            eng.matmul(wk[(0, 5)[c % 2]][:, 0:RDV], rkd[:, c, :], rvt[:, c, :], start=True, stop=True)\
                               .then_inc(rkv_ps.sem, 1)
                            dst = wk[4 if c < 2 else 1][:, (c % 2) * RDV:(c % 2 + 1) * RDV]
                            eng.matmul(dst, rsc[:, c, :], rvt[:, c, :], start=True, stop=(cc == 0))
                            if cc:
                                eng.wait_ge(rst_ok.sem, rst_ok.after(t, cc))
                                mm = eng.matmul(dst, rqd[:, c, :], rstate[:, cc % 2, :], start=False, stop=True)
                            else:
                                mm = eng.matmul(dst, rsc[:, c, :], rvt[:, c, :], start=True, stop=True)
                            mm.then_inc(ro_ps.sem, 1)
                            fill(1 if c < CPH - 1 else 8)
                        for _ in fills:
                            pass
                        eng.wait_ge(ron_ok.sem, ron_ok.after(t, hf + 1))
                        for e in range(2):
                            turn(2 + e, [ron[:, c, e * P:(e + 1) * P] for c in range(CPH)]).then_inc(rob_ps.sem, 1)

                for j in range(KT):
                    dense(n + BLK_UPR + j, (BLK_UPR + j) % 2, o_hi, o_lo,
                          ready=(lambda k: (ol_ok[k % 2].sem, ol_ok[k % 2].after(l * 2 + 1, k // 2 + 1))) if j == 0 else None)
                for j in range(KT):
                    dense(n + BLK_OUT + j, (BLK_OUT + j) % 2, act_hi, act_lo,
                          ready=(lambda k: (yl_ok.sem, yl_ok.after(l * KT + k, 2))) if j == 0 else None)
            norm_sums(DEPTH)
            for i in range(NCH):
                if i % CPH == 0:
                    eng.wait_ge(n_full.sem, n_full.after(DEPTH, (i // CPH + 1) * KT // 2))
                for a in range(2):
                    if i >= 1:
                        eng.wait_ge(out_ok, 2 * i - 1 + a)
                    for c in range(4):
                        mm = eng.transpose(wk[a][:, c * P:(c + 1) * P], final_x[:, 4 * a + c, i * P:(i + 1) * P], ident)
                    mm.then_inc(out_ps, 1)

        @block.scalar
        def _(eng):
            def squares(t, k):
                eng.wait_ge(n_add.sem, n_add.after(t, k - 1))
                eng.activation(nsq[:, k % 2, :], o_all[:, k, :], ACT.Square).then_inc(n_sq.sem, 1)

            def norm_root(t):
                for b in range(NHALF):
                    seg = slice(b * HALF, (b + 1) * HALF)
                    eng.wait_ge(n_step.sem, n_step.after(t, b + 1))
                    eng.activation(r0[:, seg], ms[:, seg], ACT.Ln).then_inc(n_act.sem, 1)
                    eng.wait_ge(n_act.sem, n_act.after(t, 2 * b + 1))
                    eng.activation(r1[:, seg], r0[:, seg], ACT.Exp, scale=-0.5).then_inc(n_act.sem, 1)

            eng.wait_ge(xin_ok, 2 * NCH)
            for k in range(KT):
                squares(0, k)
            with eng.Fori(0, DEPTH) as lay:
                l = eng.snap(lay)
                n = eng.snap(lay * NBLK)
                norm_root(l)
                for k in range(KT):
                    eng.wait_ge(n_full.sem, n_full.after(l, k + 1))
                    eng.activation(act_hi[:, k, :], hfull[:, k % HBUF, :], ACT.Copy).then_inc(n_hi.sem, 1)
                for b in range(NHALF):
                    eng.wait_ge(dense_ok[b].sem, dense_ok[b].after(n + BLK_BA, 2))
                    eng.activation(ba[:, b * HALF:(b + 1) * HALF], dense_ps[0:16, b, :], ACT.Copy)\
                       .then_inc(b_row.sem, 1)
                    eng.wait_ge(b_row.sem, b_row.after(l, b + 1))
                    eng.sem_inc(dense_free[b].sem, 2)
                eng.wait_ge(b_in.sem, b_in.after(l, 32))
                eng.activation(abias[:, 2, :], abias[:, 1, :], ACT.Exp).then_inc(b_act.sem, 1)
                eng.wait_ge(b_dve.sem, b_dve.after(l, 2))
                eng.activation(sp[:, 1, :], sp[:, 0, :], ACT.Abs).then_inc(b_act.sem, 1)
                eng.wait_ge(b_act.sem, b_act.after(l, 2))
                eng.activation(sp[:, 2, :], sp[:, 1, :], ACT.Exp, scale=-1.0).then_inc(b_act.sem, 1)
                eng.wait_ge(b_act.sem, b_act.after(l, 3))
                eng.activation(sp[:, 1, :], sp[:, 2, :], ACT.Ln, bias=ones[:, 0:1]).then_inc(b_act.sem, 1)
                eng.activation(sp[:, 3, :].rearrange("p (h c) -> p h c", h=DH),
                               btk[:, :, 0:DH].rearrange("p c h -> p h c"), ACT.Tanh, scale=0.5).then_inc(b_act.sem, 1)
                eng.wait_ge(b_gcps.sem, b_gcps.after(l, 1))
                eng.activation(sp[:, 0, :].rearrange("p (h c) -> p h c", h=DH),
                               wk[4][:, 0:64].rearrange("p (c h) -> p h c", h=DH), ACT.Exp).then_inc(b_act.sem, 1)
                eng.activation(small[:, 1, :, :], wk[4][:, 0:64].rearrange("p (c h) -> p h c", h=DH), ACT.Copy)\
                   .then_inc(b_act.sem, 1)
                eng.wait_ge(b_dve.sem, b_dve.after(l, 8))
                eng.activation(small[:, 3, :, :], sp[:, 2, :].rearrange("p (h c) -> p h c", h=DH), ACT.Exp)\
                   .then_inc(b_act.sem, 1)

                def raw_evac(g, t, first, b, buf):
                    eng.wait_ge(dense_ok[b].sem, dense_ok[b].after(g, 1))
                    eng.wait_ge(conv_s.sem, conv_s.after(t, 8 if first == 4 else 0))
                    eng.activation(raw[:, buf, 3 + b * HALF:3 + (b + 1) * HALF], dense_ps[:, b, :], ACT.Copy)\
                       .then_inc(raw_ok.sem, 1)
                    eng.wait_ge(raw_ok.sem, raw_ok.after(t, first + b + 1))
                    eng.sem_inc(dense_free[b].sem, 1)

                def kqv_tanh(t, j, b):
                    i = 2 * j + b
                    eng.wait_ge(conv_s.sem, conv_s.after(t, 4 * (i + 1)))
                    eng.wait_ge(kqv_ok.sem, kqv_ok.after(t, i - 1))
                    eng.wait_ge(sz_ok.sem, sz_ok.after(t, 0))
                    eng.activation(th[:, b, :], acc[:, b, :], ACT.Tanh, scale=0.5).then_inc(th_ok.sem, 1)

                t0r = eng.snap(l * DH)
                for j, buf in ((0, 0), (1, 1), (2, 0)):
                    for b in range(NHALF):
                        raw_evac(n + BLK_KVQ0 + j, t0r, 2 * j, b, buf)
                        if (j, b) != (2, 1):
                            kqv_tanh(t0r, j, b)

                def delta_head(h, last):
                    t = eng.snap(l * DH + h)
                    m = eng.snap(n + h * 6)

                    def finish_half(hf, i):
                        j, b = i // 2, i % 2
                        g = m + (BLK_HEADS + 3 * hf + j)
                        if hf == 0:
                            eng.wait_ge(dense_ok[b].sem, dense_ok[b].after(g, 1))
                            if j == 0:
                                eng.wait_ge(sz_ok.sem, sz_ok.after(t, 0))
                                eng.wait_ge(kqv_ok.sem, kqv_ok.after(t, 5 + b))
                                eng.activation(th[:, b, :], dense_ps[:, b, :], ACT.Tanh, scale=0.5)\
                                   .then_inc(th_ok.sem, 1)
                            else:
                                eng.wait_ge(gt_st[b].sem, gt_st[b].after(t, 16 * (j - 1)))
                                eng.activation(gate_t[:, b, :], dense_ps[:, b, :], ACT.Tanh, scale=0.5)\
                                   .then_inc(gt_ok.sem, 1)
                                eng.wait_ge(gt_ok.sem, gt_ok.after(t, 2 * (j - 1) + b + 1))
                                eng.sem_inc(dense_free[b].sem, 1)
                                eng.dma_start(gate_dram[j - 1, bass.ds(h, 1), :, b * HALF:(b + 1) * HALF]
                                              .rearrange("k p t -> p (k t)"), gate_t[:, b, :])\
                                   .then_inc(gt_st[b].sem, 16)
                        else:
                            raw_evac(g, t + 1, 2 * j, b, (0, 1, 0)[j])

                    for hf in range(NHALF):
                        for step in deltanet_schedule(hf, 16 * (3 if hf == 0 or not last else 0)):
                            what = step[0]
                            if what == "evac":
                                finish_half(hf, step[1])
                            elif what == "tanh":
                                kqv_tanh(t if hf == 0 else t + 1, step[1] // 2, step[1] % 2)
                            elif what == "tokens":
                                eng.wait_ge(sqr_ok.sem, sqr_ok.after(t, 2 * hf))
                                for a in range(2):
                                    eng.wait_ge(kq_ps.sem, kq_ps.after(t, 2 * hf + a + 1))
                                    eng.activation(sq[:, a, :], wk[3 * a][:, :], ACT.Square).then_inc(sq_ok.sem, 1)
                                eng.wait_ge(row_in[0].sem, row_in[0].after(t, 16 * hf + 16))
                                eng.wait_ge(st_ok.sem, st_ok.after(t, CPH * hf))
                                eng.wait_ge(qd_ok.sem, qd_ok.after(t, hf))
                                eng.activation(egc.rearrange("p c t -> p (c t)"), gcb, ACT.Exp).then_inc(egc_ok.sem, 1)
                                eng.wait_ge(dif_ok.sem, dif_ok.after(t, 2 * hf + 2))
                                eng.wait_ge(aT_ok.sem, aT_ok.after(t, hf))
                                eng.activation(dec, t0, ACT.Exp).then_inc(dec_ok.sem, 1)
                            elif what == "khat_back":
                                eng.wait_ge(khb_ps.sem, khb_ps.after(t, hf + 1))
                                eng.activation(khT, chunks(2), ACT.Copy).then_inc(khT_ok.sem, 1)
                            elif what in ("x_first", "inv_x"):
                                i = 0 if what == "x_first" else step[1] + 1
                                if i == 0:
                                    eng.wait_ge(og_s.sem, og_s.after(t, 4 * hf))
                                for c in (0, 2):
                                    eng.wait_ge(x_ps.sem, x_ps.after(t, pair(6 * hf + i, c)))
                                    eng.activation(xx[:, c:c + 2, :], pair_of(X_BANKS, c), ACT.Copy)\
                                       .then_inc(x_ok.sem, 1)
                            elif what == "w":
                                eng.wait_ge(w_ps.sem, w_ps.after(t, hf + 1))
                                eng.activation(nw, chunks(3), ACT.Copy, scale=-1.0).then_inc(nw_ok.sem, 1)
                            elif what == "state_out" and step[1] == CPH - 1:
                                eng.wait_ge(o_ps.sem, o_ps.after(t, CPH * hf + CPH))
                                eng.activation(xx, chunks(1), ACT.Square).then_inc(osq_ok.sem, 1)


                with eng.Fori(0, DH - 1) as h:
                    delta_head(h, False)
                delta_head(DH - 1, True)

                def merge_streams(a):
                    if a == 0:
                        for b in range(NHALF):
                            eng.wait_ge(gt_st[b].sem, gt_st[b].after(l * DH + DH - 1, 32))
                        eng.wait_ge(ob_ok.sem, ob_ok.after(l * DH + DH - 1, 2))
                    else:
                        for b in range(NHALF):
                            eng.wait_ge(y_st[b].sem, y_st[b].after(l * KT + KT - 1, 16))
                        eng.wait_ge(rob_ok.sem, rob_ok.after(l * RH + RH - 1, 4))
                    for k in range(KT):
                        eng.activation(o_hi[:, k, :], o_all[:, k, :], ACT.Copy).then_inc(oh_ok.sem, 1)
                    for j in range(KT):
                        g = l * (2 * KT) + (a * KT + j)
                        for b in range(NHALF):
                            seg = slice(b * HALF, (b + 1) * HALF)
                            eng.wait_ge(yg_ok.sem, yg_ok.after(g, b - 1))
                            eng.dma_start(gy[:, b, :], gate_dram[a, j, :, seg]).then_inc(g_in[b].sem, 16)
                            if a:
                                eng.wait_ge(yf_ok.sem, yf_ok.after(l * KT + j, b - 1))
                                eng.dma_start(y1[:, b, :], y_dram[j, :, seg]).then_inc(y_in[b].sem, 16)
                        if a == 0:
                            for b in range(NHALF):
                                eng.wait_ge(yg_ok.sem, yg_ok.after(g, b + 1))
                                eng.dma_start(y_dram[j, :, b * HALF:(b + 1) * HALF], y1[:, b, :])\
                                   .then_inc(y_st[b].sem, 16)

                merge_streams(0)
                for b in range(NHALF):
                    eng.wait_ge(y_st[b].sem, y_st[b].after(l * KT + KT - 1, 16))
                eng.dma_start(rope_t, rope.rearrange("p (a t) -> p a t", a=2)).then_inc(rope_in.sem, 16)
                with eng.Fori(0, RH) as h:
                    t = eng.snap(l * RH + h)
                    m = eng.snap(n + h * 6)
                    for j in range(2):
                        for b in range(NHALF):
                            eng.wait_ge(dense_ok[b].sem, dense_ok[b].after(m + BLK_RET + j, 1))
                            eng.wait_ge(rrot.sem, rrot.after(t, 4 * j + 2 * b - 2))
                            for s in range(2):
                                eng.activation(swap[64 * s:64 * s + 64, b, :],
                                               dense_ps[64 - 64 * s:128 - 64 * s, b, :], ACT.Copy)\
                                   .then_inc(swap_ok.sem, 1)
                    for e in range(2):
                        for b in range(NHALF):
                            eng.wait_ge(dense_ok[b].sem, dense_ok[b].after(m + BLK_RET + 2 + e, 1))
                            eng.wait_ge(rtok_ps.sem, rtok_ps.after(t, 0))
                            eng.activation(rvT[:, e, b * HALF:(b + 1) * HALF], dense_ps[:, b, :], ACT.Copy)\
                               .then_inc(rv_ok.sem, 1)
                            eng.wait_ge(rv_ok.sem, rv_ok.after(t, 2 * e + b + 1))
                            eng.sem_inc(dense_free[b].sem, 1)
                    for hf in range(NHALF):
                        eng.wait_ge(rtok_ps.sem, rtok_ps.after(t, 2 * hf + 2))
                        eng.wait_ge(ro_ps.sem, ro_ps.after(t, CPH * hf))
                        for e in range(2):
                            eng.activation(rvt[:, :, e * P:(e + 1) * P], chunks(2 + e), ACT.Copy).then_inc(rvt_ok.sem, 1)
                        for e in range(2):
                            eng.wait_ge(dense_ok[hf].sem, dense_ok[hf].after(m + BLK_RET + 4 + e, 1))
                            eng.wait_ge(rsz_ok.sem, rsz_ok.after(t, 2 * hf + e - 1))
                            eng.activation(rth[:, e, :], dense_ps[:, hf, :], ACT.Tanh, scale=0.5).then_inc(rth_ok.sem, 1)

                merge_streams(1)
                eng.wait_ge(yf_ok.sem, yf_ok.after(l * KT + KT - 1, 2))
                eng.wait_ge(x0_stored, 16)
                eng.wait_ge(xn_st.sem, xn_st.after(l, 0))
                for j in range(KT):
                    for b in range(NHALF):
                        eng.wait_ge(xn_ok.sem, xn_ok.after(l * KT + j, b - 1))
                        eng.dma_start(y1[:, b, :], x_dram[j, :, b * HALF:(b + 1) * HALF]).then_inc(xo_in[b].sem, 16)
                    if j:
                        squares(l + 1, j - 1)
                eng.wait_ge(xn_ok.sem, xn_ok.after(l * KT + KT - 1, 2))
                squares(l + 1, KT - 1)
            norm_root(DEPTH)
            for i in range(NCH):
                eng.wait_ge(out_ps, NCH + 2 * i + 1)
                if i >= 2:
                    eng.wait_ge(out_stored[i % 2], 16 * (i // 2))
                eng.activation(xin[:, i % 2, 0:HALF], wk[0][:, :], ACT.Copy).then_inc(out_ok, 1)
                eng.wait_ge(out_ps, NCH + 2 * i + 2)
                eng.wait_ge(out_ok, 2 * i + 1)
                eng.activation(xin[:, i % 2, HALF:SEQ], wk[1][:, :], ACT.Copy).then_inc(out_ok, 1)

        @block.vector
        def _(eng):
            def split_w(g, slot, inc=1):
                eng.wait_ge(w_in_ok.sem, w_in_ok.after(g, 16 * inc))
                eng.wait_ge(dense_ok[1].sem, dense_ok[1].after(g, -1))
                eng.tensor_copy(w_hi[:, slot, :, :], w_raw[:, :, :]).then_inc(w_hi_ok.sem, inc)

            def norm_apply(t, final):
                for b in range(NHALF):
                    eng.wait_ge(n_ps.sem, n_ps.after(t, b + 1))
                    eng.tensor_scalar(ms[:, b * HALF:(b + 1) * HALF], wk[b][:, :], 1.0 / D_MODEL, EPS,
                                      ALU.mult, ALU.add).then_inc(n_step.sem, 1)
                for b in range(NHALF):
                    ra, rb, mb = (v[:, b * HALF:(b + 1) * HALF] for v in (r0, r1, ms))
                    eng.wait_ge(n_act.sem, n_act.after(t, 2 * b + 2))
                    eng.tensor_tensor(ra, rb, rb, ALU.mult).then_inc(n_step.sem, 1)
                    eng.wait_ge(n_step.sem, n_step.after(t, 4 * b + 3))
                    eng.scalar_tensor_tensor(out=ra, in0=ra, scalar=-0.5, in1=mb, op0=ALU.mult, op1=ALU.mult)\
                       .then_inc(n_step.sem, 1)
                    eng.wait_ge(n_step.sem, n_step.after(t, 4 * b + 4))
                    eng.scalar_tensor_tensor(out=rb, in0=ra, scalar=1.5, in1=rb, op0=ALU.add, op1=ALU.mult)\
                       .then_inc(n_step.sem, 2)
                eng.wait_ge(n_step.sem, n_step.after(t, 10))
                if final:
                    for b in range(NHALF):
                        seg = slice(b * HALF, (b + 1) * HALF)
                        for k in range(KT):
                            ins = eng.scalar_tensor_tensor(out=final_x[:, k, seg], in0=o_all[:, k, seg],
                                                           scalar=cols[:, ROW_FG + k:ROW_FG + k + 1],
                                                           in1=r1[:, seg], op0=ALU.mult, op1=ALU.mult)
                            if k % 2:
                                ins.then_inc(n_full.sem, 1)
                    return
                for k in range(KT):
                    gain = cols[:, ROW_NG + k:ROW_NG + k + 1]
                    eng.wait_ge(n_lo[k % 2].sem, n_lo[k % 2].after(t, (k - HBUF) // 2 + 1))
                    eng.scalar_tensor_tensor(out=hfull[:, k % HBUF, :], in0=o_all[:, k, :], scalar=gain, in1=r1,
                                             op0=ALU.mult, op1=ALU.mult).then_inc(n_full.sem, 1)
                    if k >= 2 and k % 2 == 0:
                        norm_lo(t, k - 1)
                norm_lo(t, KT - 1)

            def norm_lo(t, k):
                eng.wait_ge(n_hi.sem, n_hi.after(t, k + 1))
                eng.tensor_tensor(act_lo[:, k, :], hfull[:, k % HBUF, :], act_hi[:, k, :].bitcast(F32), ALU.subtract)\
                   .then_inc(n_lo[1].sem, 1)

            def add_squares(t, k):
                eng.wait_ge(n_sq.sem, n_sq.after(t, k + 1))
                if k == 0:
                    eng.tensor_copy(ssq, nsq[:, 0, :]).then_inc(n_add.sem, 1)
                else:
                    eng.wait_ge(n_add.sem, n_add.after(t, k))
                    eng.tensor_tensor(ssq, ssq, nsq[:, k % 2, :], ALU.add).then_inc(n_add.sem, 1)

            for i in range(NCH):
                for a in range(2):
                    eng.wait_ge(*((out_ps, i + 1) if a == 0 else (xin_ps, i + 1)))
                    eng.tensor_copy(o_all[:, 4 * a:4 * a + 4, i * P:(i + 1) * P], chunks(a)).then_inc(xin_ok, 1)

            for k in range(KT):
                add_squares(0, k)

            with eng.Fori(0, DEPTH) as lay:
                l = eng.snap(lay)
                n = eng.snap(lay * NBLK)
                eng.wait_ge(cols_ps, l + 1)
                eng.tensor_copy(cols[:, 0:ROWS], wk[2][:, 0:ROWS]).then_inc(cols_ok, 1)
                eng.wait_ge(cols_ok, l * 2 + 1)
                eng.tensor_scalar(dngh[:, :], cols[:, ROW_DN:ROW_DN + 1], 0.5, None, ALU.mult).then_inc(cols_ok, 1)
                split_w(n + BLK_BA, 0, 2)
                norm_apply(l, False)
                for lo in n_lo:
                    eng.wait_ge(lo.sem, lo.after(l, KT // 2))
                eng.memset(raw[:, :, 0:3], 0.0).then_inc(halo_ok.sem, 1)
                split_w(n + BLK_KVQ0, 0)
                eng.wait_ge(b_tokps.sem, b_tokps.after(l, 1))
                eng.tensor_copy(btk, wk[3][:, 0:P].rearrange("p (c n) -> p c n", c=NCH)).then_inc(b_dve.sem, 1)
                eng.wait_ge(b_dve.sem, b_dve.after(l, 1))
                eng.wait_ge(b_in.sem, b_in.after(l, 32))
                split_w(n + BLK_KVQ0 + 1, 1)
                z3 = sp[:, 0, :].rearrange("p (c h) -> p c h", h=DH)
                eng.tensor_tensor(z3, btk[:, :, DH:16], abias[:, 0, :].unsqueeze(1).to_broadcast([P, NCH, DH]), ALU.add)\
                   .then_inc(b_dve.sem, 1)
                eng.wait_ge(b_act.sem, b_act.after(l, 4))
                eng.scalar_tensor_tensor(out=sp[:, 2, :], in0=sp[:, 0, :], scalar=0.0, in1=sp[:, 1, :],
                                         op0=ALU.max, op1=ALU.add).then_inc(b_dve.sem, 1)
                eng.wait_ge(b_dve.sem, b_dve.after(l, 3))
                eng.scalar_tensor_tensor(out=g_tok[:, :, :], in0=sp[:, 2, :].rearrange("p (c h) -> p c h", h=DH),
                                         scalar=-1.0, in1=abias[:, 2, :].unsqueeze(1).to_broadcast([P, NCH, DH]),
                                         op0=ALU.mult, op1=ALU.mult).then_inc(b_dve.sem, 1)
                eng.wait_ge(b_act.sem, b_act.after(l, 5))
                eng.tensor_scalar(small[:, 0, :, :], sp[:, 3, :].rearrange("p (h c) -> p h c", h=DH), 0.5, 0.5,
                                  ALU.mult, ALU.add).then_inc(b_dve.sem, 2)
                eng.wait_ge(b_act.sem, b_act.after(l, 7))
                eng.wait_ge(b_dve.sem, b_dve.after(l, 6))
                eng.tensor_tensor(small[:, 2, :, :], small[:, 0, :, :],
                                  sp[:, 0, :].rearrange("p (h c) -> p h c", h=DH), ALU.mult).then_inc(b_dve.sem, 1)
                eng.tensor_tensor(sp[:, 2, :].rearrange("p (h c) -> p h c", h=DH),
                                  wk[4][:, 64:128].rearrange("p (c h) -> p h c", h=DH), small[:, 1, :, :],
                                  ALU.subtract).then_inc(b_dve.sem, 1)
                for a in range(2):
                    eng.wait_ge(b_rowps.sem, b_rowps.after(l, a + 1))
                    eng.tensor_copy(rows8[:, a, 0:HALF], wk[0][0:DH, :])
                    eng.tensor_copy(rows8[:, a, HALF:SEQ], wk[1][0:DH, :]).then_inc(b_rows.sem, 1)

                def conv(t, h, j, b, buf, taps=range(TAPS)):
                    i = 2 * j + b
                    which = (1, 2, 0)[j]
                    slot = (0, 2, 1)[j]
                    if 0 in taps:
                        eng.wait_ge(raw_ok.sem, raw_ok.after(t, i + 1))
                        eng.wait_ge(kqv_ok.sem, kqv_ok.after(t, i - 1))
                    for k in taps:
                        src = raw[:, buf, k + b * HALF:k + (b + 1) * HALF]
                        wcol = cols[:, bass.ds(ROW_CONV + 24 * k + 8 * which + h, 1)]
                        if k == 0:
                            eng.tensor_scalar(acc[:, b, :], src, wcol, None, ALU.mult).then_inc(conv_s.sem, 1)
                        else:
                            eng.wait_ge(conv_s.sem, conv_s.after(t, 4 * i + k))
                            eng.scalar_tensor_tensor(out=acc[:, b, :], in0=src, scalar=wcol, in1=acc[:, b, :],
                                                     op0=ALU.mult, op1=ALU.add).then_inc(conv_s.sem, 1)

                def silu(t, j, b):
                    i = 2 * j + b
                    slot = (0, 2, 1)[j]
                    eng.wait_ge(th_ok.sem, th_ok.after(t, i + 1))
                    if j != 2:
                        eng.wait_ge(tok_ps.sem, tok_ps.after(t, 0))
                    else:
                        eng.wait_ge(gram_ps.sem, gram_ps.after(t, 0))
                        eng.wait_ge(qd_ok.sem, qd_ok.after(t, 0))
                    eng.scalar_tensor_tensor(out=kqv[:, slot, b * HALF:(b + 1) * HALF], in0=th[:, b, :], scalar=1.0,
                                             in1=acc[:, b, :], op0=ALU.add, op1=ALU.mult).then_inc(kqv_ok.sem, 1)

                t0r = eng.snap(l * DH)
                for j, buf in ((0, 0), (1, 1), (2, 0)):
                    for b in range(NHALF):
                        if b == 0 and j < 2:
                            split_w(n + BLK_KVQ0 + j + 2, j % 2)
                        if (j, b) != (2, 1):
                            conv(t0r, 0, j, b, buf)
                            silu(t0r, j, b)

                def delta_head(h, last):
                    t = eng.snap(l * DH + h)
                    m = eng.snap(n + h * 6)
                    eng.wait_ge(b_act.sem, b_act.after(l, 8))
                    eng.wait_ge(kw_ok.sem, kw_ok.after(t, 0))
                    eng.wait_ge(kd_ok.sem, kd_ok.after(t, 0))
                    eng.tensor_copy(hs, small[:, :, bass.ds(h, 1), :].rearrange("p a h c -> p a (h c)"))\
                       .then_inc(hs_ok.sem, 1)

                    def z_silu(b):
                        eng.wait_ge(th_ok.sem, th_ok.after(t, 6 + b + 1))
                        eng.wait_ge(ob_ok.sem, ob_ok.after(t, 0))
                        eng.scalar_tensor_tensor(out=sz[:, b * HALF:(b + 1) * HALF], in0=th[:, b, :], scalar=1.0,
                                                 in1=dense_ps[:, b, :], op0=ALU.add, op1=ALU.mult)\
                           .then_inc(sz_ok.sem, 1)
                        eng.wait_ge(sz_ok.sem, sz_ok.after(t, b + 1))
                        eng.sem_inc(dense_free[b].sem, 1)

                    for hf in range(NHALF):
                        cs = slice(CPH * hf, CPH * hf + CPH)

                        def per_token(ap):
                            return ap.unsqueeze(2).to_broadcast([P, CPH, P])

                        for step in deltanet_schedule(hf, 16 * (3 if hf == 0 or not last else 0)):
                            what = step[0]
                            if what == "split":
                                idx = BLK_HEADS + 3 * hf + step[1] + 1
                                split_w(m + idx, idx % 2)
                            elif what == "z_silu":
                                z_silu(step[1])
                            elif what == "conv":
                                j, b = step[1] // 2, step[1] % 2
                                conv(t if hf == 0 else t + 1, h if hf == 0 else h + 1, j, b, (0, 1, 0)[j], (step[2],))
                            elif what == "silu":
                                silu(t if hf == 0 else t + 1, step[1] // 2, step[1] % 2)
                            elif what == "tokens":
                                def row_norms(a):
                                    eng.wait_ge(sq_ok.sem, sq_ok.after(t, 2 * hf + a + 1))
                                    part = slice(CPH * a, CPH * a + CPH)
                                    eng.tensor_reduce(ssum[:, part], sq[:, a, :].rearrange("p (c t) -> p c t", c=CPH),
                                                      mybir.AxisListType.X, ALU.add).then_inc(sqr_ok.sem, 1)
                                    eng.wait_ge(sqr_ok.sem, sqr_ok.after(t, 2 * hf + a + 1))
                                    eng.tensor_scalar(nrm[:, 2 * hf, part], ssum[:, part], 0.25, EPS, ALU.mult,
                                                      ALU.add).then_inc(nrm_s.sem, 1)

                                row_norms(0)
                                eng.wait_ge(tok_ps.sem, tok_ps.after(t, hf + 1))
                                if hf == 0:
                                    eng.wait_ge(hs_ok.sem, hs_ok.after(t, 1))
                                eng.scalar_tensor_tensor(out=vb, in0=chunks(4), scalar=0.5,
                                                         in1=per_token(hs[:, 0, cs]), op0=ALU.mult, op1=ALU.mult)\
                                   .then_inc(vb_ok.sem, 1)
                                eng.wait_ge(nrm_p.sem, nrm_p.after(t, 2 * hf + 1))
                                eng.scalar_tensor_tensor(out=kh, in0=chunks(0), scalar=0.5,
                                                         in1=per_token(nrm[:, 2 * hf + 1, 0:CPH]), op0=ALU.mult, op1=ALU.mult)\
                                   .then_inc(kh_ok.sem, 1)
                                row_norms(1)
                            elif what == "grams":
                                eng.wait_ge(gram_ps.sem, gram_ps.after(t, hf + 1))
                                eng.wait_ge(decb_ok.sem, decb_ok.after(t, hf + 1))
                                eng.wait_ge(dm_ok.sem, dm_ok.after(t, hf + 1))
                                for c in (0, 2):
                                    cp = slice(c, c + 2)
                                    eng.tensor_tensor(t0[:, cp, :], chunks(5)[:, cp, :], yy[:, cp, :], ALU.mult)\
                                       .then_inc(l1_ok.sem, 1)
                                    eng.wait_ge(l1_ok.sem, l1_ok.after(t, pair(hf, c)))
                                    eng.tensor_tensor(xT[:, cp, :], t0[:, cp, :], ident2, ALU.add).then_inc(xT_ok.sem, 1)
                                eng.tensor_tensor(lT, chunks(5), decb, ALU.mult).then_inc(lT_ok.sem, 1)
                                eng.tensor_tensor(aT, chunks(4), dec, ALU.mult).then_inc(aT_ok.sem, 1)
                            elif what == "inv_y":
                                i = step[1]
                                level = mk[:, C_LV + i * P:C_LV + (i + 1) * P].unsqueeze(1).to_broadcast([P, 2, P])
                                for c in (0, 2):
                                    eng.wait_ge(y_ps.sem, y_ps.after(t, pair(6 * hf + i, c)))
                                    eng.tensor_tensor(yy[:, c:c + 2, :], pair_of(Y_BANKS, c), level, ALU.mult)\
                                       .then_inc(y_ok.sem, 1)
                            elif what == "inv_xt":
                                i = step[1]
                                for c in (0, 2):
                                    cp = slice(c, c + 2)
                                    eng.wait_ge(xt_ps.sem, xt_ps.after(t, pair(6 * hf + i, c)))
                                    eng.tensor_tensor(xT[:, cp, :], xT[:, cp, :], pair_of(XT_BANKS, c), ALU.subtract)\
                                       .then_inc(xT_ok.sem, 1)
                            elif what == "v_new":
                                c = step[1]
                                cc = CPH * hf + c
                                eng.wait_ge(vn_ps.sem, vn_ps.after(t, cc + 1))
                                eng.tensor_copy(vn[:, c % 2, :], wk[4][:, (c % 2) * P:(c % 2 + 1) * P])\
                                   .then_inc(vn_ok.sem, 1)
                            elif what == "state_out":
                                c = step[1]
                                cc = CPH * hf + c
                                eng.wait_ge(st_ps.sem, st_ps.after(t, cc + 1))
                                src = wk[5][:, (c % 2) * P:(c % 2 + 1) * P]
                                if cc == 0:
                                    eng.tensor_copy(state[:, 1, :], src).then_inc(st_ok.sem, 1)
                                else:
                                    eng.wait_ge(o_ps.sem, o_ps.after(t, cc))
                                    eng.wait_ge(st_ok.sem, st_ok.after(t, cc))
                                    eng.scalar_tensor_tensor(out=state[:, (cc + 1) % 2, :], in0=state[:, cc % 2, :],
                                                             scalar=egc[:, c, P - 1:P], in1=src, op0=ALU.mult,
                                                             op1=ALU.add).then_inc(st_ok.sem, 1)
                                if c == CPH - 1:
                                    k = 4 * hf
                                    pq = nrm[:, 2 * hf + 1, CPH:8]
                                    eng.wait_ge(nrm_p.sem, nrm_p.after(t, 2 * hf + 2))
                                    eng.wait_ge(osq_ok.sem, osq_ok.after(t, hf + 1))
                                    eng.tensor_reduce(og[:, 0, :], xx, mybir.AxisListType.X, ALU.add).then_inc(og_s.sem, 1)
                                    eng.tensor_tensor(og[:, 1, :], pq, pq, ALU.mult).then_inc(og_s.sem, 1)
                                    eng.wait_ge(og_s.sem, og_s.after(t, k + 2))
                                    eng.tensor_tensor(og[:, 2, :], og[:, 0, :], og[:, 1, :], ALU.mult).then_inc(og_s.sem, 1)
                                    eng.wait_ge(og_s.sem, og_s.after(t, k + 3))
                                    eng.tensor_scalar(og[:, 3, :], og[:, 2, :], 0.25 / (DK * DK), EPS, ALU.mult, ALU.add)\
                                       .then_inc(og_s.sem, 1)
                                    eng.wait_ge(og_p.sem, og_p.after(t, hf + 1))
                                    eng.scalar_tensor_tensor(out=og[:, 5, :], in0=og[:, 4, :], scalar=0.5 * DK ** -0.5,
                                                             in1=pq, op0=ALU.mult, op1=ALU.mult).then_inc(rgl.sem, 1)
                                    eng.wait_ge(rgl.sem, rgl.after(t, hf + 1))
                                    eng.tensor_tensor(on, chunks(1), per_token(og[:, 5, :]), ALU.mult)\
                                       .then_inc(on_ok.sem, 1)
                            elif what == "o_back":
                                eng.wait_ge(ob_ps.sem, ob_ps.after(t, hf + 1))
                                eng.scalar_tensor_tensor(
                                    out=o_all[:, bass.ds(h, 1), hf * HALF:(hf + 1) * HALF].rearrange("p k t -> p (k t)"),
                                    in0=wk[1][:, :], scalar=dngh[:, 0:1], in1=sz[:, hf * HALF:(hf + 1) * HALF],
                                    op0=ALU.mult, op1=ALU.mult).then_inc(ob_ok.sem, 1)

                with eng.Fori(0, DH - 1) as h:
                    delta_head(h, False)
                delta_head(DH - 1, True)

                def merge(a):
                    for k in range(1, KT, 2):
                        eng.wait_ge(oh_ok.sem, oh_ok.after(l * 2 + a, k + 1))
                        eng.tensor_tensor(o_lo[:, k, :], o_all[:, k, :], o_hi[:, k, :].bitcast(F32), ALU.subtract)\
                           .then_inc(ol_ok[1].sem, 1)
                    for j in range(KT):
                        idx = (BLK_UPR if a else BLK_UPD) + j
                        split_w(n + idx + 1, (idx + 1) % 2)
                        g = l * (2 * KT) + (a * KT + j)
                        for b in range(NHALF):
                            eng.wait_ge(dense_ok[b].sem, dense_ok[b].after(n + idx, 1))
                            eng.wait_ge(g_in[b].sem, g_in[b].after(g, 16))
                            if a == 0:
                                eng.wait_ge(y_st[b].sem, y_st[b].after(l * KT + j, 0))
                                eng.scalar_tensor_tensor(out=y1[:, b, :], in0=gy[:, b, :], scalar=1.0,
                                                         in1=dense_ps[:, b, :], op0=ALU.add, op1=ALU.mult)\
                                   .then_inc(yg_ok.sem, 1)
                                eng.wait_ge(yg_ok.sem, yg_ok.after(g, b + 1))
                                eng.sem_inc(dense_free[b].sem, 1)
                            else:
                                eng.wait_ge(yl_ok.sem, yl_ok.after(l * KT + j, b - 1))
                                eng.scalar_tensor_tensor(out=yf[:, b, :], in0=gy[:, b, :], scalar=1.0,
                                                         in1=dense_ps[:, b, :], op0=ALU.add, op1=ALU.mult)\
                                   .then_inc(yg_ok.sem, 1)
                                eng.wait_ge(yg_ok.sem, yg_ok.after(g, b + 1))
                                eng.sem_inc(dense_free[b].sem, 1)
                                eng.wait_ge(y_in[b].sem, y_in[b].after(l * KT + j, 16))
                                eng.tensor_tensor(yf[:, b, :], yf[:, b, :], y1[:, b, :], ALU.add).then_inc(yf_ok.sem, 1)
                                eng.wait_ge(yf_ok.sem, yf_ok.after(l * KT + j, b + 1))
                                eng.tensor_copy(act_hi[:, j, b * HALF:(b + 1) * HALF], yf[:, b, :]).then_inc(yh_ok.sem, 1)

                merge(0)

                with eng.Fori(0, RH) as h:
                    t = eng.snap(l * RH + h)
                    m = eng.snap(n + h * 6)
                    eng.wait_ge(rope_in.sem, rope_in.after(l, 16))
                    for j in range(2):
                        split_w(m + BLK_RET + j + 1, (BLK_RET + j + 1) % 2)
                        for b in range(NHALF):
                            i = 2 * j + b
                            seg = slice(b * HALF, (b + 1) * HALF)
                            eng.wait_ge(swap_ok.sem, swap_ok.after(t, 2 * i + 2))
                            eng.wait_ge(rpart.sem, rpart.after(t, i))
                            eng.tensor_tensor(rt1, dense_ps[:, b, :], rope_t[:, 0, seg], ALU.mult).then_inc(rrot.sem, 1)
                            eng.tensor_tensor(rt2, swap[:, b, :], rope_t[:, 1, seg], ALU.mult).then_inc(rrot.sem, 1)
                            eng.wait_ge(rrot.sem, rrot.after(t, 2 * i + 2))
                            eng.sem_inc(dense_free[b].sem, 1)
                            eng.tensor_tensor(rkq[:, j, seg], rt1, rt2, ALU.add).then_inc(rpart.sem, 1)
                    split_w(m + BLK_RET + 3, (BLK_RET + 3) % 2)
                    split_w(m + BLK_RET + 4, (BLK_RET + 4) % 2)
                    split_w(m + BLK_RET + 5, (BLK_RET + 5) % 2)

                    def z_silu(hf, e):
                        eng.wait_ge(rth_ok.sem, rth_ok.after(t, 2 * hf + e + 1))
                        eng.scalar_tensor_tensor(out=rsz[:, e, hf * HALF:(hf + 1) * HALF], in0=rth[:, e, :],
                                                 scalar=1.0, in1=dense_ps[:, hf, :], op0=ALU.add, op1=ALU.mult)\
                           .then_inc(rsz_ok.sem, 1)
                        eng.wait_ge(rsz_ok.sem, rsz_ok.after(t, 2 * hf + e + 1))
                        eng.sem_inc(dense_free[hf].sem, 1)

                    for hf in range(NHALF):
                        seg = slice(hf * HALF, (hf + 1) * HALF)
                        eng.wait_ge(rc_in.sem, rc_in.after(t, 16))
                        eng.wait_ge(ro_ps.sem, ro_ps.after(t, CPH * hf))
                        eng.wait_ge(rpart.sem, rpart.after(t, 4))
                        eng.tensor_tensor(rqd, rkq[:, 1, seg].rearrange("p (c t) -> p c t", c=CPH),
                                          bcast4(rcon[:, P:2 * P]), ALU.mult).then_inc(rqd_ok.sem, 1)
                        eng.wait_ge(rtok_ps.sem, rtok_ps.after(t, 2 * hf + 1))
                        eng.tensor_scalar(rkd, chunks(0), rcon[:, 2 * P:2 * P + 1], None, ALU.mult)\
                           .then_inc(rkd_ok.sem, 1)
                        eng.wait_ge(rsc_ps.sem, rsc_ps.after(t, hf + 1))
                        eng.tensor_tensor(rsc, chunks(1), bcast4(rcon[:, 0:P]), ALU.mult).then_inc(rsc_ok.sem, 1)
                        for c in range(CPH):
                            cc = CPH * hf + c
                            eng.wait_ge(rkv_ps.sem, rkv_ps.after(t, cc + 1))
                            src = wk[(0, 5)[c % 2]][:, 0:RDV]
                            if cc == 0:
                                eng.tensor_copy(rstate[:, 1, :], src).then_inc(rst_ok.sem, 1)
                            else:
                                eng.wait_ge(ro_ps.sem, ro_ps.after(t, cc))
                                eng.wait_ge(rst_ok.sem, rst_ok.after(t, cc))
                                eng.scalar_tensor_tensor(out=rstate[:, (cc + 1) % 2, :], in0=rstate[:, cc % 2, :],
                                                         scalar=rcon[:, 2 * P + 1:2 * P + 2], in1=src,
                                                         op0=ALU.mult, op1=ALU.add).then_inc(rst_ok.sem, 1)
                            if c == CPH - 2:
                                z_silu(hf, 0)
                        for c in range(CPH):
                            o_src = wk[4 if c < 2 else 1][:, (c % 2) * RDV:(c % 2 + 1) * RDV]
                            eng.wait_ge(ro_ps.sem, ro_ps.after(t, CPH * hf + 2 * (c // 2) + 2))
                            eng.bn_stats(bst[:, c, :], o_src).then_inc(rbn.sem, 1)
                        for c in range(CPH):
                            eng.wait_ge(rbn.sem, rbn.after(t, 10 * hf + c + 1))
                            settled(eng)
                            eng.bn_aggr(bmv[:, c, :], bst[:, c, :]).then_inc(rbn.sem, 1)
                        eng.wait_ge(rbn.sem, rbn.after(t, 10 * hf + 8))
                        eng.tensor_scalar(brs[:, 0, :], bmv[:, :, 1], EPS, None, ALU.add).then_inc(rbn.sem, 2)
                        if hf == 1:
                            split_w(m + BLK_RET + 6, (BLK_RET + 6) % 2)
                        eng.wait_ge(rpw.sem, rpw.after(t, hf + 1))
                        for c in range(CPH):
                            o_src = wk[4 if c < 2 else 1][:, (c % 2) * RDV:(c % 2 + 1) * RDV]
                            ins = eng.tensor_scalar(ron[:, c, :], o_src, bmv[:, c, 0:1], brs[:, 1, c:c + 1],
                                                    ALU.subtract, ALU.mult)
                        ins.then_inc(ron_ok.sem, 1)
                        z_silu(hf, 1)
                        for e in range(2):
                            eng.wait_ge(rob_ps.sem, rob_ps.after(t, 2 * hf + e + 1))
                            eng.scalar_tensor_tensor(
                                out=o_all[:, bass.ds(h * 2 + e, 1), seg].rearrange("p k t -> p (k t)"),
                                in0=wk[2 + e][:, :], scalar=0.5, in1=rsz[:, e, seg],
                                op0=ALU.mult, op1=ALU.mult).then_inc(rob_ok.sem, 1)

                merge(1)

                for j in range(KT):
                    idx = BLK_OUT + j
                    if j < KT - 1:
                        split_w(n + idx + 1, (idx + 1) % 2)
                    for b in range(NHALF):
                        eng.wait_ge(dense_ok[b].sem, dense_ok[b].after(n + idx, 1))
                        eng.wait_ge(xo_in[b].sem, xo_in[b].after(l * KT + j, 16))
                        if j == 0:
                            for lo in ol_ok:
                                eng.wait_ge(lo.sem, lo.after(l * 2 + 1, KT // 2))
                        eng.scalar_tensor_tensor(out=o_all[:, j, b * HALF:(b + 1) * HALF], in0=dense_ps[:, b, :],
                                                 scalar=0.5, in1=y1[:, b, :], op0=ALU.mult, op1=ALU.add)\
                           .then_inc(xn_ok.sem, 1)
                        eng.wait_ge(xn_ok.sem, xn_ok.after(l * KT + j, b + 1))
                        eng.sem_inc(dense_free[b].sem, 1)
                    if j:
                        add_squares(l + 1, j - 1)
                add_squares(l + 1, KT - 1)
            norm_apply(DEPTH, True)

        @block.gpsimd
        def _(eng):
            def split_w(g, slot, inc=1):
                eng.wait_ge(w_hi_ok.sem, w_hi_ok.after(g, inc))
                eng.tensor_tensor(w_lo[:, slot, :, :], w_raw[:, :, :], w_hi[:, slot, :, :].bitcast(F32), ALU.subtract)\
                   .then_inc(w_lo_ok.sem, inc)

            eng.memset(negh[:, :], -0.5).then_inc(pool_set, 1)
            eng.wait_ge(pool_set, 1)
            with eng.Fori(0, DEPTH) as lay:
                l = eng.snap(lay)
                n = eng.snap(lay * NBLK)
                split_w(n + BLK_BA, 0, 2)
                for k in range(0, KT, 2):
                    eng.wait_ge(n_hi.sem, n_hi.after(l, k + 1))
                    eng.tensor_tensor(act_lo[:, k, :], hfull[:, k % HBUF, :], act_hi[:, k, :].bitcast(F32),
                                      ALU.subtract).then_inc(n_lo[0].sem, 1)
                split_w(n + BLK_KVQ0, 0)
                for j in range(3):
                    split_w(n + BLK_KVQ0 + j + 1, (j + 1) % 2)

                def delta_head(h, last):
                    t = eng.snap(l * DH + h)
                    m = eng.snap(n + h * 6)

                    for hf in range(NHALF):
                        cs = slice(CPH * hf, CPH * hf + CPH)

                        def per_token(ap):
                            return ap.unsqueeze(2).to_broadcast([P, CPH, P])

                        gcb3 = gcb.rearrange("p (c t) -> p c t", c=CPH)
                        for step in deltanet_schedule(hf, 16 * (3 if hf == 0 or not last else 0)):
                            what = step[0]
                            if what == "split":
                                idx = BLK_HEADS + 3 * hf + step[1] + 1
                                split_w(m + idx, idx % 2)
                            elif what == "tokens":
                                eng.wait_ge(row_in[0].sem, row_in[0].after(t, 16 * hf + 16))
                                eng.wait_ge(xT_ok.sem, xT_ok.after(t, 2 * (7 * hf - 6)))
                                eng.tensor_tensor(t0, gcb3, bcast4(mk[:, C_NEG:C_NEG + P]), ALU.add)\
                                   .then_inc(dif_ok.sem, 1)
                                eng.wait_ge(hs_ok.sem, hs_ok.after(t, 1))
                                eng.wait_ge(dif_ok.sem, dif_ok.after(t, 2 * hf + 1))
                                eng.tensor_tensor(t0, t0, per_token(hs[:, 1, cs]), ALU.subtract)\
                                   .then_inc(dif_ok.sem, 1)
                                def power(a):
                                    part = slice(CPH * a, CPH * a + CPH)
                                    eng.wait_ge(nrm_s.sem, nrm_s.after(t, 2 * hf + a + 1))
                                    eng.wait_ge(on_ok.sem, on_ok.after(t, hf))
                                    eng.tensor_tensor(nrm[:, 2 * hf + 1, part], nrm[:, 2 * hf, part],
                                                      negh[:, 0:CPH], ALU.pow).then_inc(nrm_p.sem, 1)

                                power(0)
                                eng.wait_ge(dec_ok.sem, dec_ok.after(t, hf + 1))
                                eng.wait_ge(row_in[1].sem, row_in[1].after(t, 16 * hf + 16))
                                eng.tensor_tensor(decb, dec, beb.rearrange("p (c t) -> p c t", c=CPH), ALU.mult)\
                                   .then_inc(decb_ok.sem, 1)
                                eng.wait_ge(decb_ok.sem, decb_ok.after(t, hf + 1))
                                eng.wait_ge(xt_ps.sem, xt_ps.after(t, 12 * hf))
                                eng.tensor_tensor(yy, decb, bcast4(mk[:, C_M1:C_M1 + P]), ALU.mult)\
                                   .then_inc(dm_ok.sem, 1)
                                eng.wait_ge(egc_ok.sem, egc_ok.after(t, hf + 1))
                                eng.wait_ge(o_ps.sem, o_ps.after(t, CPH * hf))
                                eng.tensor_tensor(qd, kqv[:, 1, hf * HALF:(hf + 1) * HALF]
                                                  .rearrange("p (c t) -> p c t", c=CPH), egc, ALU.mult)\
                                   .then_inc(qd_ok.sem, 1)
                                power(1)
                                eng.wait_ge(kh_ok.sem, kh_ok.after(t, hf + 1))
                                eng.tensor_tensor(kw, kh, per_token(hs[:, 2, cs]), ALU.mult).then_inc(kw_ok.sem, 1)
                                eng.tensor_tensor(kd, kh, per_token(hs[:, 3, cs]), ALU.mult).then_inc(kd_ok.sem, 1)
                            elif what == "state_out" and step[1] == CPH - 1:
                                eng.wait_ge(og_s.sem, og_s.after(t, 4 * hf + 4))
                                eng.tensor_tensor(og[:, 4, :], og[:, 3, :], negh[:, 0:CPH], ALU.pow).then_inc(og_p.sem, 1)

                with eng.Fori(0, DH - 1) as h:
                    delta_head(h, False)
                delta_head(DH - 1, True)

                def merge(a):
                    for k in range(0, KT, 2):
                        eng.wait_ge(oh_ok.sem, oh_ok.after(l * 2 + a, k + 1))
                        eng.tensor_tensor(o_lo[:, k, :], o_all[:, k, :], o_hi[:, k, :].bitcast(F32), ALU.subtract)\
                           .then_inc(ol_ok[0].sem, 1)
                    for j in range(KT):
                        idx = (BLK_UPR if a else BLK_UPD) + j
                        split_w(n + idx + 1, (idx + 1) % 2)
                        if a:
                            for b in range(NHALF):
                                seg = slice(b * HALF, (b + 1) * HALF)
                                eng.wait_ge(yh_ok.sem, yh_ok.after(l * KT + j, b + 1))
                                eng.tensor_tensor(act_lo[:, j, seg], yf[:, b, :], act_hi[:, j, seg].bitcast(F32),
                                                  ALU.subtract).then_inc(yl_ok.sem, 1)

                merge(0)
                with eng.Fori(0, RH) as h:
                    t = eng.snap(l * RH + h)
                    m = eng.snap(n + h * 6)
                    for j in range(5):
                        split_w(m + BLK_RET + j + 1, (BLK_RET + j + 1) % 2)
                    for hf in range(NHALF):
                        eng.wait_ge(rbn.sem, rbn.after(t, 10 * hf + 10))
                        eng.tensor_tensor(brs[:, 1, :], brs[:, 0, :], negh[:, 0:CPH], ALU.pow).then_inc(rpw.sem, 1)
                        if hf == 1:
                            split_w(m + BLK_RET + 6, (BLK_RET + 6) % 2)
                merge(1)
                for j in range(KT - 1):
                    split_w(n + BLK_OUT + j + 1, (BLK_OUT + j + 1) % 2)


_INS = ["x", "norm_gain", "w_in", "conv_w", "a_log", "dt_bias", "dn_norm_gain", "w_up_ret", "w_up_dn", "w_out",
        "final_gain"]


def kernel(**inputs):
    import concourse.bacc as bacc
    from concourse.bass_utils import run_bass_kernel_spmd

    nc = bacc.Bacc("TRN2", target_bir_lowering=False, num_devices=1)
    arrays, args = {}, []
    given = {name: np.ascontiguousarray(inputs[name]) for name in _INS}
    given.update(constants())
    for name, a in given.items():
        arrays[f"in_{name}"] = a
        args.append(nc.dram_tensor(f"in_{name}", a.shape, mybir.dt.from_np(a.dtype), kind="ExternalInput").ap())
    out = nc.dram_tensor("out_0", [1, SEQ, D_MODEL], F32, kind="ExternalOutput").ap()
    build(nc, *args, out)
    r = run_bass_kernel_spmd(nc, [arrays], core_ids=[0])
    return r.results[0]["out_0"]
```
